# Optimizing a Trainium2 kernel written in Bass

```python
import math
import jax, jax.numpy as jnp
from jax import lax
import numpy as np

D_MODEL = 1024
BATCH = 1
SEQ = 256
DEPTH = 1

POOL_WIDTH = 512
POOL_WINDOWS = (2, 4, 8, 16)
POOL_GROUPS = len(POOL_WINDOWS)
POOL_GROUP_WIDTH = POOL_WIDTH // POOL_GROUPS
N_HEADS = 8
HEAD_DIM = 64
ATTN_WIDTH = N_HEADS * HEAD_DIM
N_IDX_HEADS = 4
IDX_DIM = 64
IDX_SCALE = (IDX_DIM ** -0.5) * (N_IDX_HEADS ** -0.5)
ATTN_SCALE = HEAD_DIM ** -0.5
TOPK_MAX = 256
Q_BLOCK = 128
REL_BUCKETS = 32
REL_MAX_DIST = 128
N_BRANCHES = 2
N_EXPERTS = 32
TOP_K_EXPERTS = 4
D_FF = D_MODEL
SWIGLU_LIMIT = 7.0
SWIGLU_ALPHA = 1.702
RMS_EPS = 1e-5
NEG_BIG = -1e30
SPLIT_SIZES = (POOL_WIDTH, ATTN_WIDTH, ATTN_WIDTH, ATTN_WIDTH,
               N_IDX_HEADS * IDX_DIM, IDX_DIM, N_IDX_HEADS, N_BRANCHES * D_MODEL)
D_IN = sum(SPLIT_SIZES)

kernel_name = "hybrid_pool_dsa_gated_moe_block"

def rmsnorm(x, g):
    xf = x.astype(jnp.float32)
    y = xf * lax.rsqrt(jnp.mean(xf * xf, axis=-1, keepdims=True) + RMS_EPS)
    return (y * g.astype(jnp.float32)).astype(x.dtype)

def pool_mixer(u, w_grp, scale):
    b, s, _ = u.shape
    uf = u.astype(jnp.float32).reshape(b, s, POOL_GROUPS, POOL_GROUP_WIDTH)
    csum = lax.cumsum(uf, axis=1)
    t = jnp.arange(s)
    outs = []
    for g, w in enumerate(POOL_WINDOWS):
        cg = csum[:, :, g]
        shifted = jnp.pad(cg, ((0, 0), (w, 0), (0, 0)))[:, :s]
        cnt = jnp.minimum(t + 1, w).astype(jnp.float32)[None, :, None]
        outs.append((cg - shifted) / cnt - uf[:, :, g])
    pooled = jnp.stack(outs, axis=2)
    mixed = jnp.einsum('bsgc,gcd->bsgd', pooled, w_grp.astype(jnp.float32))
    mixed = mixed * scale.astype(jnp.float32).reshape(POOL_GROUPS, POOL_GROUP_WIDTH)
    return mixed.reshape(b, s, POOL_WIDTH).astype(u.dtype)

def rel_bucket(dist):
    n = jnp.maximum(dist, 0)
    max_exact = REL_BUCKETS // 2
    nf = jnp.maximum(n, 1).astype(jnp.float32)
    large = max_exact + (jnp.log(nf / max_exact) / math.log(REL_MAX_DIST / max_exact)
                         * (REL_BUCKETS - max_exact)).astype(jnp.int32)
    large = jnp.minimum(large, REL_BUCKETS - 1)
    return jnp.where(n < max_exact, n, large)

def dsa_attention(q, k, v, qi, ki, wi, rel_table):
    b, s = q.shape[0], q.shape[1]
    topk = min(TOPK_MAX, s // 4)
    nb = s // Q_BLOCK
    key_pos = jnp.arange(s)
    ki_f = ki.astype(jnp.float32)
    table = rel_table.astype(jnp.float32)
    gather = jax.vmap(lambda a, i: a[i])

    def to_blocks(a):
        return a.reshape((b, nb, Q_BLOCK) + a.shape[2:]).swapaxes(0, 1)

    def block_fn(args):
        qb, qib, wib, start = args
        t = start + jnp.arange(Q_BLOCK)
        sc = jnp.einsum('bqhd,bsd->bqhs', qib.astype(jnp.float32), ki_f)
        score = jnp.einsum('bqhs,bqh->bqs', jax.nn.relu(sc), wib.astype(jnp.float32)) * IDX_SCALE
        causal = key_pos[None, :] <= t[:, None]
        score = jnp.where(causal[None], score, -jnp.inf)
        _, idx = lax.top_k(score, topk)
        valid = idx <= t[None, :, None]
        k_sel = gather(k, idx).astype(jnp.float32)
        v_sel = gather(v, idx).astype(jnp.float32)
        logits = jnp.einsum('bqhd,bqkhd->bqhk', qb.astype(jnp.float32), k_sel) * ATTN_SCALE
        bias = table[rel_bucket(t[None, :, None] - idx)]
        logits = logits + bias.transpose(0, 1, 3, 2)
        logits = jnp.where(valid[:, :, None, :], logits, NEG_BIG)
        p = jax.nn.softmax(logits, axis=-1)
        out = jnp.einsum('bqhk,bqkhd->bqhd', p, v_sel)
        return out.astype(q.dtype)

    starts = jnp.arange(nb, dtype=jnp.int32) * Q_BLOCK
    outs = lax.map(block_fn, (to_blocks(q), to_blocks(qi), to_blocks(wi), starts))
    return outs.swapaxes(0, 1).reshape(b, s, ATTN_WIDTH)

def moe(h, w_router, b_router, w1, b1, w2, b2):
    b, s, d = h.shape
    hf = h.reshape(b * s, d)
    logits = hf.astype(jnp.float32) @ w_router.astype(jnp.float32) + b_router.astype(jnp.float32)
    top_vals, top_idx = lax.top_k(logits, TOP_K_EXPERTS)
    gates = jax.nn.softmax(top_vals, axis=-1)
    combine = jnp.sum(jax.nn.one_hot(top_idx, N_EXPERTS, dtype=jnp.float32) * gates[..., None], axis=1)
    out = jnp.zeros((b * s, d), jnp.float32)
    for e in range(N_EXPERTS):
        gu = hf @ w1[e] + b1[e]
        g_ = jnp.minimum(gu[:, :D_FF].astype(jnp.float32), SWIGLU_LIMIT)
        u_ = jnp.clip(gu[:, D_FF:].astype(jnp.float32), -SWIGLU_LIMIT, SWIGLU_LIMIT)
        act = (g_ * jax.nn.sigmoid(SWIGLU_ALPHA * g_) * (u_ + 1.0)).astype(h.dtype)
        out = out + combine[:, e:e + 1] * (act @ w2[e] + b2[e]).astype(jnp.float32)
    return out.reshape(b, s, d).astype(h.dtype)

def setup_inputs(seed: int = 0) -> dict:
    key = jax.random.key(seed)
    ks = jax.random.split(key, 20)
    f32 = jnp.float32
    nrm = lambda k, shape, sc: jax.random.normal(k, shape, f32) * sc
    return {
        "x": nrm(ks[0], (BATCH, SEQ, D_MODEL), 1.0),
        "mix_norm": 1.0 + nrm(ks[1], (DEPTH, D_MODEL), 0.02),
        "w_in": nrm(ks[2], (DEPTH, D_MODEL, D_IN), D_MODEL ** -0.5),
        "pool_w": nrm(ks[3], (DEPTH, POOL_GROUPS, POOL_GROUP_WIDTH, POOL_GROUP_WIDTH), POOL_GROUP_WIDTH ** -0.5),
        "pool_scale": 1.0 + nrm(ks[4], (DEPTH, POOL_WIDTH), 0.1),
        "w_branch_pool": nrm(ks[5], (DEPTH, POOL_WIDTH, D_MODEL), POOL_WIDTH ** -0.5),
        "w_branch_attn": nrm(ks[6], (DEPTH, ATTN_WIDTH, D_MODEL), ATTN_WIDTH ** -0.5),
        "rel_bias": nrm(ks[7], (REL_BUCKETS, N_HEADS), 0.5),
        "w_out": nrm(ks[8], (DEPTH, D_MODEL, D_MODEL), D_MODEL ** -0.5),
        "ffn_norm": 1.0 + nrm(ks[9], (DEPTH, D_MODEL), 0.02),
        "w_router": nrm(ks[10], (DEPTH, D_MODEL, N_EXPERTS), D_MODEL ** -0.5),
        "b_router": nrm(ks[11], (DEPTH, N_EXPERTS), 0.01),
        "w1": nrm(ks[12], (DEPTH, N_EXPERTS, D_MODEL, 2 * D_FF), D_MODEL ** -0.5),
        "b1": nrm(ks[13], (DEPTH, N_EXPERTS, 2 * D_FF), 0.01),
        "w2": nrm(ks[14], (DEPTH, N_EXPERTS, D_FF, D_MODEL), D_FF ** -0.5),
        "b2": nrm(ks[15], (DEPTH, N_EXPERTS, D_MODEL), 0.01),
        "final_norm": 1.0 + nrm(ks[16], (D_MODEL,), 0.02),
    }

def reference(x, mix_norm, w_in, pool_w, pool_scale, w_branch_pool, w_branch_attn, rel_bias,
              w_out, ffn_norm, w_router, b_router, w1, b1, w2, b2, final_norm):
    b, s, _ = x.shape
    offsets = [int(o) for o in np.cumsum(SPLIT_SIZES)[:-1]]
    for l in range(DEPTH):
        h = rmsnorm(x, mix_norm[l])
        z = h @ w_in[l]
        z_pool, z_q, z_k, z_v, z_qi, z_ki, z_wi, z_gate = jnp.split(z, offsets, axis=-1)
        y_pool = pool_mixer(z_pool, pool_w[l], pool_scale[l]) @ w_branch_pool[l]
        q = z_q.reshape(b, s, N_HEADS, HEAD_DIM)
        k = z_k.reshape(b, s, N_HEADS, HEAD_DIM)
        v = z_v.reshape(b, s, N_HEADS, HEAD_DIM)
        qi = z_qi.reshape(b, s, N_IDX_HEADS, IDX_DIM)
        y_attn = dsa_attention(q, k, v, qi, z_ki, z_wi, rel_bias) @ w_branch_attn[l]
        gates = jax.nn.sigmoid(z_gate.astype(jnp.float32)).reshape(b, s, N_BRANCHES, D_MODEL)
        merged = gates[:, :, 0] * y_pool.astype(jnp.float32) + gates[:, :, 1] * y_attn.astype(jnp.float32)
        x = x + merged.astype(x.dtype) @ w_out[l]
        h2 = rmsnorm(x, ffn_norm[l])
        x = x + moe(h2, w_router[l], b_router[l], w1[l], b1[l], w2[l], b2[l])
    return rmsnorm(x, final_norm)


_drawn_inputs = setup_inputs


def setup_inputs(seed=0):
    import zlib

    import numpy as np

    out = dict(_drawn_inputs(seed))
    spreads = {}
    factors = {'b1': 8.0, 'b2': 8.0, 'final_norm': 2.854}
    for name, (base, spread) in spreads.items():
        noise = np.random.default_rng([zlib.crc32(name.encode()), seed]).standard_normal(out[name].shape)
        drawn = base * np.exp(spread * noise) if base else spread * noise
        out[name] = __import__('jax').numpy.asarray(drawn.astype(out[name].dtype))
    for name, factor in factors.items():
        out[name] = (out[name] * factor).astype(out[name].dtype)
    return out
```

```python
import concourse.bass as bass
from concourse import mybir
from contextlib import ExitStack
import math
import numpy as np

P = 128
SEQ, D = 256, 1024
TB = SEQ // P
KD = D // P
HALF = 512
POOL_WINDOWS = (2, 4, 8, 16)
NH, DH = 8, 64
NIH, DI = 4, 64
TOPK = SEQ // 4
BUCKETS, MAX_DIST = 32, 128
NE, TOPE = 32, 4
F = D
LIMIT, ALPHA, EPS = 7.0, 1.702, 1e-5
NEG_BIG = -1e30
MASKED, TAKEN = -3.0e38, -3.3e38
SLOTS = 64
ROUNDS = SEQ // SLOTS

C_POOL, C_Q, C_K, C_V = 0, 512, 1024, 1536
C_QI = 2048
C_GATE = C_QI + NIH * DI + DI + NIH
N_IDX = NIH * DI + DI + NIH

RING = 12
SLOT = 2048
CHUNKS = 12
G_IDX, G_Q, G_K, G_V, G_POOL, G_GATE = 0, 2, 4, 6, 8, 10
U_BP, U_BA, U_WO = 18, 20, 22
FRONT_USES = 26

K_ID, K_TRI, K_ONE, K_FLIP, K_IOTA, K_BAND = 0, 128, 256, 384, 512, 576
N_CONST = K_BAND + 12 * 128
R_MASK, R_COMB, R_COUNT = 5, 9, 11
SKEW = 384


def hybrid_block(nc, x, mix_norm, w_in, pool_w, pool_scale, w_bp, w_ba, rel_bias, w_out,
                 ffn_norm, w_router, b_router, w1, b1, w2, b2, final_norm, consts, bucket_hot, out):
    f32, i32 = mybir.dt.float32, mybir.dt.int32
    ALU = mybir.AluOpType
    ACT = mybir.ActivationFunctionType
    X = mybir.AxisListType.X

    ctx = ExitStack()
    with ctx:
        def sb(name, shape, dt=f32):
            return ctx.enter_context(nc.sbuf_tensor(name, shape, dt))

        def sem(name):
            return ctx.enter_context(nc.semaphore(name))

        ring = sb("ring", [P, RING, SLOT])
        xs = sb("xs", [P, TB, D])
        hs = sb("hs", [P, TB, D])
        hT = sb("hT", [P, KD, SEQ])
        gmix = sb("gmix", [P, D])
        gffn = sb("gffn", [P, D])
        cst = sb("cst", [P, K_BAND])
        ident, tri = cst[:, K_ID:K_ID + P], cst[:, K_TRI:K_TRI + P]
        ones, iota1 = cst[:, K_ONE:K_ONE + P], cst[:, K_IOTA:K_IOTA + SLOTS]
        flip = cst[:, K_FLIP:K_FLIP + P]
        gates = sb("gates", [P, TB, 2 * D])
        bias_up = gates[:, 0, :].rearrange("p (h s) -> p h s", h=NH)
        keepm = sb("keepm", [P, TB, SEQ])
        wi = sb("wi", [P, TB, NIH])
        poolw = sb("poolw", [P, 4, P])
        pscale = sb("pscale", [P, 4])
        wr = sb("wr", [P, KD, NE])
        br = sb("br", [P, NE])
        table = sb("table", [BUCKETS, NH])
        stat = sb("stat", [P, 24])
        ss, var, std, rstd = stat[:, 0:2], stat[:, 2:4], stat[:, 4:6], stat[:, 6:8]
        lsum, linv, nlmax = stat[:, 8:10], stat[:, 10:12], stat[:, 12:14]
        hmax = sb("hmax", [P, 2, 2])
        nhmax = sb("nhmax", [P, 2, 2])
        hsum = sb("hsum", [P, 2, 2])
        hinv = sb("hinv", [P, 2, 2])
        m8 = sb("m8", [P, 8])
        r1 = sb("r1", [P, 8 * 1024])
        qT = r1[:, 0:1024].rearrange("p (b t) -> p b t", b=4)
        kT = r1[:, 1024:2048].rearrange("p (b t) -> p b t", b=4)
        qiT = r1[:, 2048:2560].rearrange("p (b t) -> p b t", b=2)
        kiT = r1[:, 2560:2816]
        relu = r1[:, 2816:3840].rearrange("p (r j s) -> p r j s", r=2, j=2)
        score = r1[:, 3840:4352].rearrange("p (b s) -> p b s", b=2)
        vv = r1[:, 4352:5376].rearrange("p (b c) -> p b c", b=2)
        logit = r1[:, 5376:6144].rearrange("p (r s) -> p r s", r=2)
        prob = r1[:, 6144:6912].rearrange("p (r s) -> p r s", r=2)
        pT = r1[:, 6912:7680].rearrange("p (r s) -> p r s", r=2)
        hot = r1[0:BUCKETS, 6144:6144 + SKEW]
        skew = r1[0:NH, 6144 + SKEW:6144 + 2 * SKEW]
        b1s = r1[:, 0:2048]
        b2s = r1[0:NE, 2048:3072]
        gclip = r1[:, 3072:3584]
        sig = r1[:, 3584:4096]
        uclip = r1[:, 4096:4608]
        act = r1[:, 4608:5120]
        actT = r1[:, 5120:5632]
        ys = r1[:, 5632:6144]
        xgT = r1[:, 6144:6656].rearrange("p (k s) -> p k s", k=KD)
        gT = r1[:, 6656:6912]
        pick = r1[:, 6912:7040].rearrange("p (b s) -> p b s", b=TB)
        gpick = r1[:, 7040:7296].rearrange("p (b u s) -> p b u s", b=TB, u=2)
        sel = r1[:, 7296:7360]
        combT = r1[0:NE, 7360:7616]
        iota_r = r1[:, 7616:7680]
        bias = sb("bias", [P, NH, SEQ])
        r3 = sb("r3", [P, 3584])
        uu = r3[:, 0:1024].rearrange("p (b c) -> p b c", b=2)
        pooledT = r3[:, 1024:2048].rearrange("p (g t) -> p g t", g=4)
        band = r3[:, 2048:3584].rearrange("p (m t) -> p m t", t=P)
        mixT = r3[:, 0:1024].rearrange("p (g t) -> p g t", g=4)
        attT = r3[:, 1024:2048].rearrange("p (g t) -> p g t", g=4)
        lg = r3[:, 0:80].rearrange("p (b e) -> p b e", b=2)
        lgt = r3[:, 80:160].rearrange("p (b e) -> p b e", b=2)
        top8 = r3[:, 160:176].rearrange("p (b e) -> p b e", b=2)
        rep8 = r3[:, 176:192].rearrange("p (b e) -> p b e", b=2)
        emask = r3[:, 192:256].rearrange("p (b e) -> p b e", b=2)
        eexp = r3[:, 256:320].rearrange("p (b e) -> p b e", b=2)
        comb = r3[:, 320:386].rearrange("p (b e) -> p b e", b=2)
        posn = r3[:, 386:452].rearrange("p (b e) -> p b e", b=2)
        cmax = r3[0:1, 452:453]
        count = sb("count", [1, 1], i32)

        bank = [ctx.enter_context(nc.psum_tensor(f"bank{i}", [P, HALF], f32)) for i in range(8)]
        GA, UA, GATHER, YT = bank[0:4]
        YSUM = bank[4:8]

        skew_dram = nc.dram_tensor("skew_dram", (NH, SKEW), f32, kind="Internal").ap()

        slot_loaded = [sem(f"slot_loaded{s}") for s in range(RING)]
        slots_used = sem("slots_used")
        x_loaded, cst_loaded = sem("x_loaded"), sem("cst_loaded")
        gmix_loaded, gffn_loaded, gfin_loaded = sem("gmix_loaded"), sem("gffn_loaded"), sem("gfin_loaded")
        table_loaded, band_loaded, poolw_loaded = sem("table_loaded"), sem("band_loaded"), sem("poolw_loaded")
        router_loaded, b12_loaded = sem("router_loaded"), sem("b12_loaded")
        skew_summed, skew_ready = sem("skew_summed"), sem("skew_ready")
        skew_saved, bias_loaded = sem("skew_saved"), sem("bias_loaded")
        flip_done, bias_ready = sem("flip_done"), sem("bias_ready")
        squares_ready, var_ready, std_ready = sem("squares_ready"), sem("var_ready"), sem("std_ready")
        rstd_ready = sem("rstd_ready")
        h_ready = sem("h_ready")
        tp_done, tp_evac = sem("tp_done"), sem("tp_evac")
        idx_done, idx_ready = sem("idx_done"), sem("idx_ready")
        sc_done, relu_ready, score_ready = sem("sc_done"), sem("relu_ready"), sem("score_ready")
        causal_ready, taken_ready, kept_ready = sem("causal_ready"), sem("taken_ready"), sem("kept_ready")
        keepm_ready = sem("keepm_ready")
        half_done, half_evac = sem("half_done"), sem("half_evac")
        gate_ready = sem("gate_ready")
        pool_done, pool_evac = sem("pool_done"), sem("pool_evac")
        logit_done, logit_read, logit_ready = sem("logit_done"), sem("logit_read"), sem("logit_ready")
        hmax_ready, nhmax_ready, exp_ready = sem("hmax_ready"), sem("nhmax_ready"), sem("exp_ready")
        hinv_ready, prob_ready = sem("hinv_ready"), sem("prob_ready")
        pT_done, pT_ready, pv_done, att_ready = sem("pT_done"), sem("pT_ready"), sem("pv_done"), sem("att_ready")
        branch_done, gated, merged = sem("branch_done"), sem("gated"), sem("merged")
        wo_done, x_ready = sem("wo_done"), sem("x_ready")
        router_done, routing, nlmax_ready = sem("router_done"), sem("routing"), sem("nlmax_ready")
        eexp_ready, rank_done = sem("eexp_ready"), sem("rank_done")
        combT_done, combT_ready = sem("combT_done"), sem("combT_ready")
        count_ready = sem("count_ready")
        sel_ready, b1_zeroed = sem("sel_ready"), sem("b1_zeroed")
        pick_ready, gather_done, xgT_ready = sem("pick_ready"), sem("gather_done"), sem("xgT_ready")
        gpick_ready, gT_done, gT_ready = sem("gpick_ready"), sem("gT_done"), sem("gT_ready")
        gclip_ready, sig_ready, act_ready = sem("gclip_ready"), sem("sig_ready"), sem("act_ready")
        uclip_ready, gu_ready = sem("uclip_ready"), sem("gu_ready")
        actT_done, actT_ready = sem("actT_done"), sem("actT_ready")
        y_ready, scattered = sem("y_ready"), sem("scattered")
        iota_ready = sem("iota_ready")
        out_saved = sem("out_saved")

        block = ctx.enter_context(nc.Block())

        w_in_k = w_in.rearrange("(k p) n -> p k n", p=P)
        w1_k = w1.rearrange("e (k p) n -> e p k n", p=P)
        w2_k = w2.rearrange("e (k p) n -> e p k n", p=P)

        def ring_wait(eng, use):
            eng.wait_ge(slot_loaded[use % RING], 16 * (use // RING + 1))

        def ring_wait_expert(eng, unit, j):
            s = (FRONT_USES + j) % RING
            first = (FRONT_USES + j) // RING + 1
            eng.wait_ge(slot_loaded[s], 16 * unit + 16 * first)

        def cols(g):
            return [ring[:, (g + i) % RING, :].rearrange("p (k n) -> p k n", k=4) for i in range(2)]

        def rows(u, n):
            return [ring[:, (u + i) % RING, :].rearrange("p (k n) -> p k n", k=2) for i in range(n)]

        @block.sync
        def _(sp):
            sp.dma_start(xs[:, :, :], x.rearrange("(b p) d -> p b d", p=P)).then_inc(x_loaded, 16)

            def load(use, dst, src):
                if use >= RING:
                    sp.wait_ge(slots_used, use - RING + 1)
                sp.dma_start(dst, src).then_inc(slot_loaded[use % RING], 16)

            for g, c0, n in ((G_IDX, C_QI, N_IDX), (G_Q, C_Q, 512), (G_K, C_K, 512), (G_V, C_V, 512),
                             (G_POOL, C_POOL, 512), *((G_GATE + 2 * i, C_GATE + 512 * i, 512) for i in range(4))):
                for i in range(2):
                    load(g + i, cols(g)[i][:, :, 0:n], w_in_k[:, 4 * i:4 * i + 4, c0:c0 + n])
            for u, w, n in ((U_BP, w_bp, 2), (U_BA, w_ba, 2), (U_WO, w_out, 4)):
                wk = w.rearrange("(k p) n -> p k n", p=P)
                for i in range(n):
                    load(u + i, rows(u, n)[i], wk[:, 2 * i:2 * i + 2, :])

            def load_round(r):
                with sp.Fori(0, NE) as e:
                    for j in range(CHUNKS):
                        s = (FRONT_USES + j) % RING
                        sp.wait_ge(slots_used, (r * NE + e) * CHUNKS + FRONT_USES + j - RING + 1)
                        if j < KD:
                            sp.dma_start(ring[:, s, :], w1_k[e, :, j, :]).then_inc(slot_loaded[s], 16)
                        else:
                            sp.dma_start(rows(FRONT_USES + j, 1)[0],
                                         w2_k[e, :, 2 * (j - KD):2 * (j - KD) + 2, :]).then_inc(slot_loaded[s], 16)

            load_round(0)
            sp.wait_ge(count_ready, 1)
            most = sp.value_load(count[0:1, 0:1], min_val=0, max_val=SEQ)
            with sp.If(most > SLOTS):
                with sp.Fori(1, ROUNDS) as r:
                    load_round(r)
            for b in range(TB):
                sp.wait_ge(h_ready, 4 + b + 1)
                sp.dma_start(out[b * P:(b + 1) * P, :], hs[:, b, :]).then_inc(out_saved, 16)
            sp.wait_ge(out_saved, 16 * TB)

        @block.gpsimd
        def _(pool):
            pool.wait_ge(skew_ready, 1)
            pool.dma_start(skew_dram, skew).then_inc(skew_saved, 16)
            pool.wait_ge(skew_saved, 16)
            skewed = bass.AP(tensor=skew_dram.tensor, offset=0, ap=[[1, P], [SKEW, NH], [1, SEQ]])
            pool.dma_start(bias_up, skewed).then_inc(bias_loaded, 16)
            for b in range(TB):
                n = P * (b + 1)
                pool.wait_ge(score_ready, b + 1)
                nc.gpsimd.affine_select(out=score[:, b, 0:n], in_=score[:, b, 0:n], compare_op=ALU.is_ge,
                                        fill=MASKED, base=P * b, pattern=[[-1, n]],
                                        channel_multiplier=1).then_inc(causal_ready, 1)
            for b in range(TB):
                n = P * (b + 1)
                pool.wait_ge(kept_ready, b + 1)
                nc.gpsimd.affine_select(out=keepm[:, b, 0:n], in_=keepm[:, b, 0:n], compare_op=ALU.is_ge,
                                        fill=NEG_BIG, base=P * b, pattern=[[-1, n]],
                                        channel_multiplier=1).then_inc(keepm_ready, 1)
            pool.wait_ge(h_ready, 2)
            pool.dma_start(gmix[:, :], final_norm.partition_broadcast(P)).then_inc(gfin_loaded, 16)
            pool.wait_ge(gated, 12)
            pool.wait_ge(b1_zeroed, 1)
            pool.dma_start(b1s[0:NE, :], b1).then_inc(b12_loaded, 16)
            pool.dma_start(b2s, b2).then_inc(b12_loaded, 16)

        @block.scalar
        def _(a):
            a.dma_start(cst[:, :], consts[:, 0:K_BAND]).then_inc(cst_loaded, 16)
            a.dma_start(gmix[:, :], mix_norm.partition_broadcast(P)).then_inc(gmix_loaded, 16)
            a.dma_start(hot, bucket_hot).then_inc(table_loaded, 16)
            a.dma_start(table[:, :], rel_bias).then_inc(table_loaded, 16)
            a.dma_start(band, consts[:, K_BAND:].rearrange("p (m t) -> p m t", t=P)).then_inc(band_loaded, 16)
            a.dma_start(poolw[:, :, :], pool_w.rearrange("g c d -> c g d")).then_inc(poolw_loaded, 16)
            a.dma_start(pscale[:, :], pool_scale).then_inc(poolw_loaded, 16)
            a.dma_start(gffn[:, :], ffn_norm.partition_broadcast(P)).then_inc(gffn_loaded, 16)
            a.dma_start(wr[:, :, :], w_router.rearrange("(k p) e -> p k e", p=P)).then_inc(router_loaded, 16)
            a.dma_start(br[:, :], b_router.partition_broadcast(P)).then_inc(router_loaded, 16)

            def squares(i):
                for b in range(TB):
                    if i == 0:
                        a.wait_ge(x_loaded, 16)
                    else:
                        a.wait_ge(x_ready, 4 * (i - 1) + 2 * (b + 1))
                    nc.scalar.activation(hs[:, b, :], xs[:, b, :], ACT.Square,
                                         accum_out=ss[:, b:b + 1]).then_inc(squares_ready, 1)
                a.wait_ge(var_ready, i + 1)
                nc.scalar.activation(std, var, ACT.Sqrt).then_inc(std_ready, 1)

            def evac_transposes(i):
                for j in (0, 2):
                    a.wait_ge(tp_done, 4 * i + j + 1)
                    nc.scalar.activation(hT[:, 2 * j:2 * j + 2, :],
                                         bank[j][:, :].rearrange("p (k t) -> p k t", k=2), ACT.Copy).then_inc(tp_evac, 1)

            squares(0)
            a.wait_ge(skew_summed, 1)
            nc.scalar.activation(skew, bank[7][0:NH, 0:SKEW], ACT.Copy).then_inc(skew_ready, 1)
            evac_transposes(0)
            a.wait_ge(idx_done, 1)
            nc.scalar.activation(qiT, bank[4][:, :].rearrange("p (b t) -> p b t", b=2), ACT.Copy).then_inc(idx_ready, 1)
            a.wait_ge(slots_used, G_IDX + 2)
            nc.scalar.activation(kiT, bank[5][:, 0:SEQ], ACT.Copy).then_inc(idx_ready, 1)
            nc.scalar.activation(wi[:, :, :], bank[5][:, SEQ:SEQ + 8].rearrange("p (b i) -> p b i", b=2),
                                 ACT.Copy).then_inc(idx_ready, 1)
            for b in range(TB):
                n = P * (b + 1)
                a.wait_ge(sc_done, b + 1)
                if b:
                    a.wait_ge(score_ready, 1)
                for r in range(2):
                    src = bank[4 + 2 * b + r][:, :].rearrange("p (j s) -> p j s", j=2)[:, :, 0:n]
                    nc.scalar.activation(relu[:, r, :, 0:n], src, ACT.Relu,
                                         scale=float(DI ** -0.5 * NIH ** -0.5)).then_inc(relu_ready, 1)

            def evac_half(hg):
                if hg % 2 == 0:
                    a.wait_ge(half_done, hg // 2 + 1)
                else:
                    a.wait_ge(slots_used, G_Q + 2 * (hg // 2) + 2)
                src = bank[hg % 4][:, :]
                pair = src.rearrange("p (b t) -> p b t", b=2)
                b = hg % 2
                if hg < 4:
                    nc.scalar.activation((qT if hg < 2 else kT)[:, 2 * b:2 * b + 2, :], pair, ACT.Copy)\
                      .then_inc(half_evac, 1)
                elif hg < 8:
                    nc.scalar.activation((vv if hg < 6 else uu)[:, b, :], src, ACT.Copy).then_inc(half_evac, 1)
                else:
                    c = HALF * ((hg - 8) // 2)
                    nc.scalar.activation(gates[:, b, c:c + HALF], src, ACT.Copy).then_inc(half_evac, 1)

            def pooled(i):
                a.wait_ge(pool_done, i + 1)
                nc.scalar.activation(pooledT[:, 2 * i:2 * i + 2, :],
                                     bank[4 + i][:, :].rearrange("p (g t) -> p g t", g=2), ACT.Copy)\
                  .then_inc(pool_evac, 1)

            def mixed(i):
                a.wait_ge(pool_done, 2 + i + 1)
                if i == 0:
                    a.wait_ge(poolw_loaded, 32)
                for g in (2 * i, 2 * i + 1):
                    nc.scalar.activation(mixT[:, g, :], bank[4 + i][:, (g % 2) * SEQ:(g % 2 + 1) * SEQ], ACT.Copy,
                                         scale=pscale[:, g:g + 1]).then_inc(pool_evac, 1)

            def exps(h):
                r = h % 2
                a.wait_ge(nhmax_ready, h + 1)
                if h >= 2:
                    a.wait_ge(pT_done, h - 1)
                for b, (s0, n) in enumerate(((0, P), (P, SEQ))):
                    nc.scalar.activation(prob[:, r, s0:s0 + n], logit[:, r, s0:s0 + n], ACT.Exp,
                                         bias=nhmax[:, r, b:b + 1], accum_out=hsum[:, r, b:b + 1])\
                      .then_inc(exp_ready, 1)

            def probs_transposed(h):
                r = h % 2
                a.wait_ge(pT_done, h + 1)
                if h >= 2:
                    a.wait_ge(pv_done, h - 1)
                nc.scalar.activation(pT[:, r, :], bank[4][:, 0:384], ACT.Copy).then_inc(pT_ready, 1)

            def attended(pr):
                a.wait_ge(pv_done, 2 * pr + 2)
                c = SEQ * (pr % 2)
                nc.scalar.activation(attT[:, pr, :], bank[5][:, c:c + SEQ], ACT.Copy).then_inc(att_ready, 1)

            for hg in range(6):
                evac_half(hg)
            for i in range(4):
                a.wait_ge(flip_done, i + 1)
                nc.scalar.activation(bias[:, 2 * i:2 * i + 2, :], bank[4 + i][:, :].rearrange("p (h s) -> p h s", h=2),
                                     ACT.Copy).then_inc(bias_ready, 1)
            for hg in (6, 7):
                evac_half(hg)
            for i in range(2):
                pooled(i)
            for i in range(2):
                mixed(i)
            for st in range(NH + 2):
                if st < NH:
                    exps(st)
                    evac_half(8 + st)
                if 1 <= st <= NH:
                    probs_transposed(st - 1)
                if st >= 3 and st % 2 == 1:
                    attended((st - 3) // 2)
            for b in range(TB):
                if b == 0:
                    a.wait_ge(half_evac, 16)
                nc.scalar.activation(gates[:, b, :], gates[:, b, :], ACT.Sigmoid).then_inc(gate_ready, 1)
            evac_transposes(1)
            squares(1)
            evac_transposes(2)
            a.wait_ge(nlmax_ready, 1)
            for b in range(TB):
                nc.scalar.activation(eexp[:, b, :], lg[:, b, 0:NE], ACT.Exp, bias=nlmax[:, b:b + 1])\
                  .then_inc(eexp_ready, 1)
            a.wait_ge(combT_done, 1)
            nc.scalar.activation(combT, bank[3][0:NE, 0:SEQ], ACT.Copy).then_inc(combT_ready, 1)

            def copy_xgT(gathers):
                a.wait_ge(gather_done, gathers)
                nc.scalar.activation(xgT, GATHER[:, :].rearrange("p (k s) -> p k s", k=KD), ACT.Copy)\
                  .then_inc(xgT_ready, 1)

            def experts_round(r):
                copy_xgT(r * (NE + 1) + 1)
                with a.Fori(0, NE) as e:
                    u = r * NE + e
                    a.wait_ge(gclip_ready, u + 1)
                    nc.scalar.activation(sig, gclip, ACT.Sigmoid, scale=ALPHA).then_inc(sig_ready, 1)
                    a.wait_ge(gT_done, u + 1)
                    nc.scalar.activation(gT, YT[:, 0:SEQ], ACT.Copy).then_inc(gT_ready, 1)
                    copy_xgT(r * (NE + 1) + e + 2)
                    a.wait_ge(actT_done, u + 1)
                    nc.scalar.activation(actT, GA[:, :], ACT.Copy).then_inc(actT_ready, 1)
                    a.wait_ge(slots_used, u * CHUNKS + FRONT_USES + CHUNKS)
                    nc.scalar.activation(ys, YT[:, :], ACT.Copy).then_inc(y_ready, 1)

            experts_round(0)
            a.wait_ge(count_ready, 1)
            most = a.value_load(count[0:1, 0:1], min_val=0, max_val=SEQ)
            with a.If(most > SLOTS):
                with a.Fori(1, ROUNDS) as r:
                    experts_round(r)
            squares(2)

        @block.vector
        def _(v):
            def norm(i, gain, gain_loaded):
                v.wait_ge(squares_ready, 2 * (i + 1))
                nc.vector.tensor_scalar(var, ss, 1.0 / D, EPS, ALU.mult, ALU.add).then_inc(var_ready, 1)
                v.wait_ge(std_ready, i + 1)
                nc.vector.reciprocal(rstd, std).then_inc(rstd_ready, 1)
                v.wait_ge(rstd_ready, i + 1)
                v.wait_ge(gain_loaded, 16)
                for b in range(TB):
                    nc.vector.scalar_tensor_tensor(out=hs[:, b, :], in0=xs[:, b, :], scalar=rstd[:, b:b + 1],
                                                   in1=gain[:, :], op0=ALU.mult, op1=ALU.mult).then_inc(h_ready, 1)

            def evac_transposes(i):
                for j in (1, 3):
                    v.wait_ge(tp_done, 4 * i + j + 1)
                    nc.vector.tensor_copy(hT[:, 2 * j:2 * j + 2, :],
                                          bank[j][:, :].rearrange("p (k t) -> p k t", k=2)).then_inc(tp_evac, 1)

            v.wait_ge(x_loaded, 16)
            norm(0, gmix, gmix_loaded)
            evac_transposes(0)
            steps = 0
            for b in range(TB):
                n = P * (b + 1)
                v.wait_ge(idx_ready, 3)
                v.wait_ge(relu_ready, 2 * b + 2)
                for i in range(NIH):
                    rl, w = relu[:, i % 2, i // 2, 0:n], wi[:, b, i:i + 1]
                    if i == 0:
                        ins = nc.vector.tensor_scalar(score[:, b, 0:n], rl, w, None, ALU.mult)
                    else:
                        ins = nc.vector.scalar_tensor_tensor(out=score[:, b, 0:n], in0=rl, scalar=w,
                                                             in1=score[:, b, 0:n], op0=ALU.mult, op1=ALU.add)
                    if i < NIH - 1:
                        steps += 1
                        ins.then_inc(taken_ready, 1)
                        v.wait_ge(taken_ready, steps)
                ins.then_inc(score_ready, 1)
            for b in range(TB):
                n = P * (b + 1)
                v.wait_ge(causal_ready, b + 1)
                for _ in range(TOPK // 8):
                    nc.vector.max(m8[:, :], score[:, b, 0:n]).then_inc(taken_ready, 1)
                    v.wait_ge(taken_ready, steps + 1)
                    nc.vector.match_replace(score[:, b, 0:n], m8[:, :], score[:, b, 0:n], TAKEN).then_inc(taken_ready, 1)
                    steps += 2
                    v.wait_ge(taken_ready, steps)
                nc.vector.tensor_scalar(keepm[:, b, 0:n], score[:, b, 0:n], (MASKED + TAKEN) / 2, NEG_BIG,
                                        ALU.is_ge, ALU.mult).then_inc(kept_ready, 1)

            def softmax_in(h):
                r = h % 2
                lb = bank[6 + r]
                v.wait_ge(logit_done, h + 1)
                if h >= 2:
                    v.wait_ge(exp_ready, 2 * (h - 1))
                for s0, n, c0 in ((0, P, P), (P, SEQ, 0)):
                    ins = nc.vector.scalar_tensor_tensor(out=logit[:, r, s0:s0 + n], in0=lb[:, s0:s0 + n],
                                                         scalar=float(DH ** -0.5), in1=bias[:, h, c0:c0 + n],
                                                         op0=ALU.mult, op1=ALU.add)
                ins.then_inc(logit_read, 1)
                v.wait_ge(logit_read, h + 1)
                for b, (s0, n) in enumerate(((0, P), (P, SEQ))):
                    ins = nc.vector.tensor_tensor_reduce(out=logit[:, r, s0:s0 + n], in0=logit[:, r, s0:s0 + n],
                                                         in1=keepm[:, b, 0:n], scale=1.0, scalar=-3.4e38,
                                                         op0=ALU.add, op1=ALU.max, accum_out=hmax[:, r, b:b + 1])
                    ins.then_inc(hmax_ready, 1)
                v.wait_ge(hmax_ready, 2 * h + 2)
                nc.vector.tensor_scalar(nhmax[:, r, :], hmax[:, r, :], -1.0, None, ALU.mult).then_inc(nhmax_ready, 1)

            def softmax_out(h):
                r = h % 2
                v.wait_ge(exp_ready, 2 * h + 2)
                nc.vector.reciprocal(hinv[:, r, :], hsum[:, r, :]).then_inc(hinv_ready, 1)
                v.wait_ge(hinv_ready, h + 1)
                for b, (s0, n) in enumerate(((0, P), (P, SEQ))):
                    ins = nc.vector.tensor_scalar(prob[:, r, s0:s0 + n], prob[:, r, s0:s0 + n],
                                                  hinv[:, r, b:b + 1], None, ALU.mult)
                ins.then_inc(prob_ready, 1)

            v.wait_ge(bias_ready, 4)
            v.wait_ge(keepm_ready, 2)
            for st in range(NH + 1):
                if st < NH:
                    softmax_in(st)
                if st >= 1:
                    softmax_out(st - 1)

            n_gated = 0
            for br_i in range(2):
                for b in range(TB):
                    for c in range(2):
                        if 2 * b + c < 3:
                            v.wait_ge(branch_done, 3 * br_i + 2 * b + c + 1)
                        else:
                            v.wait_ge(slots_used, (U_BP, U_BA)[br_i] + 2)
                        v.wait_ge(gate_ready, b + 1)
                        g = gates[:, b, D * br_i + HALF * c:D * br_i + HALF * (c + 1)]
                        m = hs[:, b, HALF * c:HALF * (c + 1)]
                        dst = g if br_i else m
                        nc.vector.tensor_tensor(dst, bank[4 * br_i + 2 * b + c][:, :], g, ALU.mult).then_inc(gated, 1)
                        n_gated += 1
                        if br_i:
                            v.wait_ge(gated, n_gated)
                            nc.vector.tensor_tensor(m, m, g, ALU.add).then_inc(gated, 1)
                            n_gated += 1
            nc.vector.memset(b1s, 0.0).then_inc(b1_zeroed, 1)
            evac_transposes(1)
            for b in range(TB):
                for c in range(2):
                    if 2 * b + c < 3:
                        v.wait_ge(wo_done, 2 * b + c + 1)
                    else:
                        v.wait_ge(slots_used, FRONT_USES)
                    xh = xs[:, b, HALF * c:HALF * (c + 1)]
                    nc.vector.tensor_tensor(xh, bank[4 + 2 * b + c][:, :], xh, ALU.add).then_inc(x_ready, 1)
            norm(1, gffn, gffn_loaded)
            nc.vector.memset(lg[:, :, NE:], MASKED)
            nc.vector.memset(posn[:, :, :], 0.0)
            nc.vector.memset(comb[:, :, :], 0.0)
            nc.vector.memset(rep8[:, :, :], MASKED)
            nc.vector.tensor_copy(iota_r, iota1).then_inc(iota_ready, 1)
            evac_transposes(2)
            v.wait_ge(iota_ready, 1)
            v.wait_ge(router_done, 1)
            v.wait_ge(router_loaded, 32)
            n = [0]

            def link(ins):
                ins.then_inc(routing, 1)
                n[0] += 1
                v.wait_ge(routing, n[0])

            link(nc.vector.tensor_tensor(lg[:, :, 0:NE], bank[0][:, 0:2 * NE].rearrange("p (b e) -> p b e", b=2),
                                         br[:, :].unsqueeze(1).to_broadcast([P, TB, NE]), ALU.add))
            for b in range(TB):
                ins = nc.vector.max(top8[:, b, :], lg[:, b, 0:NE])
            link(ins)
            nc.vector.tensor_scalar(nlmax, top8[:, :, 0], -1.0, None, ALU.mult).then_inc(nlmax_ready, 1)
            link(nc.vector.tensor_copy(rep8[:, :, 0:TOPE], top8[:, :, 0:TOPE]))
            for b in range(TB):
                ins = nc.vector.match_replace(lgt[:, b, :], rep8[:, b, :], lg[:, b, :], TAKEN)
            link(ins)
            link(nc.vector.tensor_scalar(emask, lgt[:, :, 0:NE], (MASKED + TAKEN) / 2, None, ALU.is_lt))
            v.wait_ge(eexp_ready, 2)
            link(nc.vector.tensor_tensor(eexp, eexp, emask, ALU.mult))
            link(nc.vector.tensor_reduce(lsum, eexp, X, ALU.add))
            link(nc.vector.reciprocal(linv, lsum))
            for b in range(TB):
                ins = nc.vector.tensor_scalar(comb[:, b, 0:NE], eexp[:, b, :], linv[:, b:b + 1], None, ALU.mult)
            link(ins)
            v.wait_ge(rank_done, 1)
            link(nc.vector.scalar_tensor_tensor(out=posn[:, :, 0:NE],
                                                in0=bank[1][:, 0:2 * NE].rearrange("p (b e) -> p b e", b=2),
                                                scalar=1.0, in1=emask, op0=ALU.add, op1=ALU.mult))
            link(nc.vector.tensor_reduce(cmax, bank[1][0:1, 2 * NE:3 * NE], X, ALU.max))
            nc.vector.tensor_copy(count[:, :], cmax).then_inc(count_ready, 1)

            def make_pick(e):
                for b in range(TB):
                    ins = nc.vector.tensor_scalar(pick[:, b, :], iota_r, posn[:, b, bass.ds(e, 1)], None, ALU.is_equal)
                ins.then_inc(pick_ready, 1)

            def make_sel(e):
                nc.vector.tensor_copy(sel, ident[:, bass.ds(e, 1)].to_broadcast([P, SLOTS])).then_inc(sel_ready, 1)

            def experts_round(r):
                first = isinstance(r, int)
                if not first:
                    v.wait_ge(scattered, r * NE)
                    nc.vector.tensor_scalar(iota_r, iota_r, float(SLOTS), None, ALU.add).then_inc(iota_ready, 1)
                    v.wait_ge(iota_ready, r + 1)
                make_pick(0)
                make_sel(0)
                with v.Fori(0, NE) as e:
                    u = r * NE + e
                    v.wait_ge(gather_done, r * (NE + 1) + e + 1)
                    for b in range(TB):
                        ins = nc.vector.tensor_scalar(gpick[:, b, :, :], iota_r.unsqueeze(1).to_broadcast([P, 2, SLOTS]),
                                                      posn[:, b, bass.ds(e, 1)], comb[:, b, bass.ds(e, 1)],
                                                      ALU.is_equal, ALU.mult)
                    ins.then_inc(gpick_ready, 1)
                    make_pick(e + 1)
                    v.wait_ge(slots_used, u * CHUNKS + FRONT_USES + KD)
                    make_sel(e + 1)
                    nc.vector.tensor_scalar(gclip, GA[:, :], LIMIT, None, ALU.min).then_inc(gclip_ready, 1)
                    nc.vector.tensor_scalar(uclip, UA[:, :], LIMIT, -LIMIT, ALU.min, ALU.max).then_inc(uclip_ready, 1)
                    v.wait_ge(uclip_ready, u + 1)
                    nc.vector.scalar_tensor_tensor(out=uclip, in0=uclip, scalar=1.0, in1=gclip,
                                                   op0=ALU.add, op1=ALU.mult).then_inc(gu_ready, 1)
                    v.wait_ge(sig_ready, u + 1)
                    v.wait_ge(gu_ready, u + 1)
                    nc.vector.tensor_tensor(act, uclip, sig, ALU.mult).then_inc(act_ready, 1)

            experts_round(0)
            v.wait_ge(scattered, NE)
            v.wait_ge(count_ready, 1)
            most = v.value_load(count[0:1, 0:1], min_val=0, max_val=SEQ)
            with v.If(most > SLOTS):
                with v.Fori(1, ROUNDS) as r:
                    experts_round(r)
                v.wait_ge(scattered, ROUNDS * NE)
            for b in range(TB):
                for c in range(2):
                    xh = xs[:, b, HALF * c:HALF * (c + 1)]
                    nc.vector.tensor_tensor(xh, YSUM[2 * b + c][:, :], xh, ALU.add).then_inc(x_ready, 1)
            norm(2, gmix, gfin_loaded)

        @block.tensor
        def _(pe):
            mm = nc.tensor.matmul

            pe.wait_ge(table_loaded, 32)
            mm(bank[7][0:NH, 0:SKEW], table[:, :], hot, start=True, stop=True).then_inc(skew_summed, 1)

            def transposes(i):
                for b in range(TB):
                    if i == 0:
                        pe.wait_ge(h_ready, b + 1)
                    elif i == 1:
                        pe.wait_ge(gated, 4 + 4 * (b + 1))
                    else:
                        pe.wait_ge(h_ready, 2 + b + 1)
                    for j in range(4):
                        for k in (2 * j, 2 * j + 1):
                            c = (k % 2) * SEQ + b * P
                            ins = nc.tensor.transpose(bank[j][:, c:c + P], hs[:, b, k * P:(k + 1) * P], ident)
                        if b == TB - 1:
                            ins.then_inc(tp_done, 1)

            def tok(k, b):
                return hT[:, k, b * P:(b + 1) * P]

            pe.wait_ge(cst_loaded, 16)
            transposes(0)
            pe.wait_ge(tp_evac, 4)
            w = cols(G_IDX)
            for i in range(2):
                ring_wait(pe, G_IDX + i)
            for b in range(2):
                for k in range(KD):
                    ins = mm(bank[4][:, b * SEQ:(b + 1) * SEQ], w[k // 4][:, k % 4, b * P:(b + 1) * P], hT[:, k, :],
                             start=k == 0, stop=k == KD - 1)
            ins.then_inc(idx_done, 1)
            for k in range(KD):
                for r in (0, DI):
                    mm(bank[5][r:r + DI, 0:SEQ], w[k // 4][:, k % 4, NIH * DI:NIH * DI + DI], hT[:, k, :],
                       start=k == 0, stop=k == KD - 1)
            for b in range(TB):
                for k in range(KD):
                    ins = mm(bank[5][:, SEQ + NIH * b:SEQ + NIH * (b + 1)], tok(k, b), w[k // 4][:, k % 4, NIH * DI + DI:N_IDX],
                             start=k == 0, stop=k == KD - 1)
                    if b == TB - 1 and k % 4 == 3:
                        ins.then_inc(slots_used, 1)
            pe.wait_ge(idx_ready, 3)
            pe.wait_ge(skew_ready, 1)
            for b in range(TB):
                for i in range(NIH):
                    r, c = DI * (i % 2), SEQ * (i // 2)
                    ins = mm(bank[4 + 2 * b + i % 2][:, c:c + P * (b + 1)], qiT[r:r + DI, i // 2, b * P:(b + 1) * P],
                             kiT[r:r + DI, 0:P * (b + 1)], start=True, stop=True)
                ins.then_inc(sc_done, 1)

            def half(hg):
                g = G_Q + 2 * (hg // 2)
                w, bk, b = cols(g), bank[hg % 4], hg % 2
                if b == 0:
                    for i in range(2):
                        ring_wait(pe, g + i)
                if hg >= 4:
                    pe.wait_ge(half_evac, hg - 3)
                for blk in ((2 * b, 2 * b + 1) if hg < 4 else (b,)):
                    for k in range(KD):
                        wk = w[k // 4][:, k % 4, :]
                        if hg < 4:
                            ins = mm(bk[:, (blk % 2) * SEQ:(blk % 2 + 1) * SEQ], wk[:, blk * P:(blk + 1) * P], hT[:, k, :],
                                     start=k == 0, stop=k == KD - 1)
                        else:
                            ins = mm(bk[:, :], tok(k, b), wk, start=k == 0, stop=k == KD - 1)
                        if b == 1 and k % 4 == 3 and blk in (1, 3):
                            if hg >= 4 or blk == 3:
                                ins.then_inc(slots_used, 1)
                if b == 0:
                    ins.then_inc(half_done, 1)

            for hg in range(6):
                half(hg)
            pe.wait_ge(bias_loaded, 16)
            pe.wait_ge(relu_ready, 4)
            for i in range(4):
                mm(bank[4 + i][:, :], flip, gates[:, 0, i * HALF:(i + 1) * HALF], start=True, stop=True)\
                    .then_inc(flip_done, 1)
            for hg in (6, 7):
                half(hg)
            pe.wait_ge(half_evac, 8)
            pe.wait_ge(band_loaded, 16)
            pe.wait_ge(bias_ready, 2)
            for g in range(4):
                ug, bk, c = slice(g * P, (g + 1) * P), bank[4 + g // 2], (g % 2) * SEQ
                mm(bk[:, c:c + P], uu[:, 0, ug], band[:, 3 * g, :], start=True, stop=True)
                mm(bk[:, c + P:c + SEQ], uu[:, 0, ug], band[:, 3 * g + 1, :], start=True, stop=False)
                ins = mm(bk[:, c + P:c + SEQ], uu[:, 1, ug], band[:, 3 * g + 2, :], start=False, stop=True)
                if g % 2:
                    ins.then_inc(pool_done, 1)
            pe.wait_ge(poolw_loaded, 32)
            for g in range(4):
                pe.wait_ge(pool_evac, 1 + g // 2)
                ins = mm(bank[4 + g // 2][:, (g % 2) * SEQ:(g % 2 + 1) * SEQ], poolw[:, g, :], pooledT[:, g, :],
                         start=True, stop=True)
                if g % 2:
                    ins.then_inc(pool_done, 1)

            def logits(h):
                r, q, bk = DH * (h % 2), h // 2, bank[6 + h % 2]
                if h < 2:
                    pe.wait_ge(bias_ready, 4)
                else:
                    pe.wait_ge(logit_read, h - 1)
                mm(bk[:, 0:P], qT[r:r + DH, q, 0:P], kT[r:r + DH, q, 0:P], start=True, stop=True)
                mm(bk[:, P:P + SEQ], qT[r:r + DH, q, P:SEQ], kT[r:r + DH, q, :], start=True, stop=True)\
                    .then_inc(logit_done, 1)

            def transpose_probs(h):
                pe.wait_ge(prob_ready, h + 1)
                if h == 0:
                    pe.wait_ge(pool_evac, 6)
                else:
                    pe.wait_ge(pT_ready, h)
                for i in range(3):
                    ins = nc.tensor.transpose(bank[4][:, i * P:(i + 1) * P], prob[:, h % 2, i * P:(i + 1) * P], ident)
                ins.then_inc(pT_done, 1)

            def values(h):
                r, pr = DH * (h % 2), h // 2
                c = SEQ * (pr % 2)
                pe.wait_ge(pT_ready, h + 1)
                if pr >= 1:
                    pe.wait_ge(att_ready, pr)
                o = bank[5][r:r + DH, :]
                mm(o[:, c:c + SEQ], vv[:, 0, h * DH:(h + 1) * DH], pT[:, h % 2, 0:SEQ], start=True, stop=False)
                mm(o[:, c + P:c + SEQ], vv[:, 1, h * DH:(h + 1) * DH], pT[:, h % 2, SEQ:SEQ + P], start=False, stop=True)\
                    .then_inc(pv_done, 1)

            for st in range(NH + 2):
                if st < NH:
                    logits(st)
                    half(8 + st)
                if 1 <= st <= NH:
                    transpose_probs(st - 1)
                if st >= 2:
                    values(st - 2)

            def product4(u, n, lhsT, banks, done):
                w = rows(u, n)
                for i in range(n):
                    ring_wait(pe, u + i)
                for q in range(4):
                    b, c = q // 2, q % 2
                    for k in range(2 * n):
                        ins = mm(banks[q][:, :], lhsT(k, b), w[k // 2][:, k % 2, c * HALF:(c + 1) * HALF],
                                 start=k == 0, stop=k == 2 * n - 1)
                        if q == 3 and k % 2 == 1:
                            ins.then_inc(slots_used, 1)
                    if q < 3:
                        ins.then_inc(done, 1)

            pe.wait_ge(half_evac, 16)
            product4(U_BP, 2, lambda k, b: mixT[:, k, b * P:(b + 1) * P], bank[0:4], branch_done)
            pe.wait_ge(att_ready, 4)
            pe.wait_ge(logit_read, NH)
            product4(U_BA, 2, lambda k, b: attT[:, k, b * P:(b + 1) * P], bank[4:8], branch_done)
            transposes(1)
            pe.wait_ge(tp_evac, 8)
            product4(U_WO, 4, tok, bank[4:8], wo_done)
            transposes(2)
            pe.wait_ge(tp_evac, 12)
            pe.wait_ge(router_loaded, 32)
            for b in range(TB):
                for k in range(KD):
                    ins = mm(bank[0][:, b * NE:(b + 1) * NE], tok(k, b), wr[:, k, :], start=k == 0, stop=k == KD - 1)
            ins.then_inc(router_done, 1)
            pe.wait_ge(routing, R_MASK)
            mm(bank[1][:, 0:NE], tri, emask[:, 0, :], start=True, stop=True)
            mm(bank[1][:, NE:2 * NE], ones, emask[:, 0, :], start=True, stop=False)
            mm(bank[1][:, NE:2 * NE], tri, emask[:, 1, :], start=False, stop=True)
            mm(bank[1][:, 2 * NE:3 * NE], ones, emask[:, 0, :], start=True, stop=False)
            mm(bank[1][:, 2 * NE:3 * NE], ones, emask[:, 1, :], start=False, stop=True).then_inc(rank_done, 1)
            pe.wait_ge(routing, R_COMB)
            for b in range(TB):
                ins = nc.tensor.transpose(bank[3][0:NE, b * P:(b + 1) * P], comb[:, b, 0:NE], ident)
            ins.then_inc(combT_done, 1)
            pe.wait_ge(combT_ready, 1)
            pe.wait_ge(b12_loaded, 32)
            pe.wait_ge(x_ready, 4)
            for b in range(TB):
                for c in range(2):
                    mm(YSUM[2 * b + c][:, :], combT[:, b * P:(b + 1) * P], b2s[:, c * HALF:(c + 1) * HALF],
                       start=True, stop=True)

            def gather():
                for k in range(KD):
                    for b in range(TB):
                        ins = mm(GATHER[:, k * SLOTS:(k + 1) * SLOTS], hs[:, b, k * P:(k + 1) * P], pick[:, b, :],
                                 start=b == 0, stop=b == TB - 1)
                ins.then_inc(gather_done, 1)

            lo, hi = slice(0, SLOTS), slice(SLOTS, 2 * SLOTS)

            def experts_round(r):
                if not isinstance(r, int):
                    pe.wait_ge(xgT_ready, r * (NE + 1))
                pe.wait_ge(pick_ready, r * (NE + 1) + 1)
                gather()
                with pe.Fori(0, NE) as e:
                    u = r * NE + e
                    pe.wait_ge(sel_ready, r * (NE + 1) + e + 1)
                    for bk, c in ((GA, 0), (UA, F)):
                        for rows_, c1 in ((lo, c), (hi, c + HALF)):
                            mm(bk[rows_, :], sel, b1s[:, c1:c1 + HALF], start=True, stop=False)
                    pe.wait_ge(xgT_ready, r * (NE + 1) + e + 1)
                    for k in range(KD):
                        ring_wait_expert(pe, u, k)
                        w = ring[:, (FRONT_USES + k) % RING, :]
                        for bk, c in ((GA, 0), (UA, F)):
                            for rows_, c1 in ((lo, c), (hi, c + HALF)):
                                ins = mm(bk[rows_, :], xgT[:, k, :], w[:, c1:c1 + HALF], start=False, stop=k == KD - 1)
                        ins.then_inc(slots_used, 1)
                    pe.wait_ge(gpick_ready, u + 1)
                    for b in range(TB):
                        ins = nc.tensor.transpose(YT[:, b * P:(b + 1) * P],
                                                  gpick[:, b, :, :].rearrange("p u s -> p (u s)"), ident)
                    ins.then_inc(gT_done, 1)
                    pe.wait_ge(pick_ready, r * (NE + 1) + e + 2)
                    gather()
                    pe.wait_ge(act_ready, u + 1)
                    for c in range(4):
                        ins = nc.tensor.transpose(GA[:, c * P:(c + 1) * P], act[:, c * P:(c + 1) * P], ident)
                    ins.then_inc(actT_done, 1)
                    pe.wait_ge(gT_ready, u + 1)
                    pe.wait_ge(actT_ready, u + 1)
                    for j in range(KD, CHUNKS):
                        ring_wait_expert(pe, u, j)
                        w = rows(FRONT_USES + j, 1)[0]
                        for i in range(2):
                            k = 2 * (j - KD) + i
                            a_k = actT[:, (k % 4) * P + (k // 4) * SLOTS:(k % 4) * P + (k // 4 + 1) * SLOTS]
                            for rows_, c1 in ((lo, 0), (hi, HALF)):
                                ins = mm(YT[rows_, :], a_k, w[:, i, c1:c1 + HALF], start=k == 0, stop=k == KD - 1)
                        ins.then_inc(slots_used, 1)
                    pe.wait_ge(y_ready, u + 1)
                    for b in range(TB):
                        for c, rows_ in enumerate((lo, hi)):
                            ins = mm(YSUM[2 * b + c][:, :], gT[rows_, b * P:(b + 1) * P], ys[rows_, :],
                                     start=False, stop=True, skip_group_check=True)
                    ins.then_inc(scattered, 1)

            pe.wait_ge(routing, R_COUNT)
            experts_round(0)
            pe.wait_ge(count_ready, 1)
            most = pe.value_load(count[0:1, 0:1], min_val=0, max_val=SEQ)
            with pe.If(most > SLOTS):
                with pe.Fori(1, ROUNDS) as r:
                    experts_round(r)


def constants():
    s = np.arange(P)[:, None]
    t = np.arange(P)[None, :]
    c = np.zeros((P, N_CONST), np.float32)
    c[:, K_ID:K_ID + P] = s == t
    c[:, K_TRI:K_TRI + P] = s < t
    c[:, K_ONE:K_ONE + P] = 1.0
    c[:, K_FLIP:K_FLIP + P] = s + t == P - 1
    c[:, K_IOTA:K_IOTA + SLOTS] = np.arange(1, SLOTS + 1)
    for g, w in enumerate(POOL_WINDOWS):
        near = (t - s >= 0) & (t - s < w)
        blocks = (near / np.minimum(t + 1, w) - (s == t),
                  (P + t - s < w) / w,
                  near / w - (s == t))
        for i, m in enumerate(blocks):
            at = K_BAND + (3 * g + i) * P
            c[:, at:at + P] = m
    return c


def bucket_rows():
    hot = np.zeros((BUCKETS, SKEW), np.float32)
    exact = BUCKETS // 2
    for c in range(SEQ):
        n = SEQ - 1 - c
        big = exact + int(np.float32(math.log(max(n, 1) / exact) / math.log(MAX_DIST / exact) * (BUCKETS - exact)))
        hot[n if n < exact else min(big, BUCKETS - 1), c] = 1.0
    return hot


def kernel(x, mix_norm, w_in, pool_w, pool_scale, w_branch_pool, w_branch_attn, rel_bias, w_out, ffn_norm,
           w_router, b_router, w1, b1, w2, b2, final_norm):
    import concourse.bacc as bacc
    from concourse.bass_utils import run_bass_kernel_spmd

    arrays = {
        "x": x[0], "mix_norm": mix_norm[0], "w_in": w_in[0], "pool_w": pool_w[0],
        "pool_scale": pool_scale[0].reshape(4, P).T, "w_branch_pool": w_branch_pool[0],
        "w_branch_attn": w_branch_attn[0], "rel_bias": rel_bias, "w_out": w_out[0],
        "ffn_norm": ffn_norm[0], "w_router": w_router[0], "b_router": b_router[0],
        "w1": w1[0], "b1": b1[0], "w2": w2[0], "b2": b2[0], "final_norm": final_norm,
        "consts": constants(), "bucket_hot": bucket_rows(),
    }
    arrays = {f"in_{n}": np.ascontiguousarray(a) for n, a in arrays.items()}
    nc = bacc.Bacc("TRN2", target_bir_lowering=False, num_devices=1)
    args = [nc.dram_tensor(n, a.shape, mybir.dt.from_np(a.dtype), kind="ExternalInput").ap() for n, a in arrays.items()]
    out = nc.dram_tensor("out", (SEQ, D), mybir.dt.float32, kind="ExternalOutput").ap()
    hybrid_block(nc, *args, out)
    r = run_bass_kernel_spmd(nc, [arrays], core_ids=[0])
    return r.results[0]["out"].reshape(1, SEQ, D)
```

```python
import concourse.bass as bass
from concourse import mybir
from contextlib import ExitStack
import math
import numpy as np

P = 128
SEQ, D = 256, 1024
TB = SEQ // P
KD = D // P
HALF = 512
POOL_WINDOWS = (2, 4, 8, 16)
NH, DH = 8, 64
NIH, DI = 4, 64
TOPK = SEQ // 4
BUCKETS, MAX_DIST = 32, 128
NE, TOPE = 32, 4
F = D
LIMIT, ALPHA, EPS = 7.0, 1.702, 1e-5
NEG_BIG = -1e30
MASKED, TAKEN = -3.0e38, -3.3e38
SLOTS = 64
ROUNDS = SEQ // SLOTS

C_POOL, C_Q, C_K, C_V = 0, 512, 1024, 1536
C_QI = 2048
C_GATE = C_QI + NIH * DI + DI + NIH
N_IDX = 3 * P

SLOT = 2048
ORDER = (0, 2, 1, 3)
FRING = 7
PIECE = SLOT // 2
LOOK = 4
N_PIECES = 52
P_IDX, P_Q, P_K, P_V, P_POOL, P_GATE, P_BP, P_BA, P_WO = 0, 4, 8, 12, 16, 20, 36, 40, 44
CHUNKS = 12
ERING = 16
GROUP = 4
TURNS = GROUP * CHUNKS // ERING

K_ID, K_TRI, K_ONE, K_IOTA, K_FOLD, K_BAND = 0, 128, 256, 384, 448, 480
N_CONST = K_BAND + 12 * 128
SKEW = 384
R_MASK, R_COMB, R_COUNT = 5, 9, 11


def hybrid_block(nc, x, mix_norm, w_in, pool_w, pool_scale, w_bp, w_ba, rel_bias, w_out,
                 ffn_norm, ffn_cols, w_router, b_router, w1, b1, w2, b2, final_norm, consts, bucket_hot, out):
    f32, f32r, i32 = mybir.dt.float32, mybir.dt.float32r, mybir.dt.int32
    ALU = mybir.AluOpType
    ACT = mybir.ActivationFunctionType
    X = mybir.AxisListType.X

    ctx = ExitStack()
    with ctx:
        def sem(name):
            return ctx.enter_context(nc.semaphore(name))

        base = -(-nc.sbuf_base // 64) * 64
        floats = (nc.sbuf_usable_end - base) // 4
        ctx.enter_context(nc.sbuf_tensor("arena", [P, (nc.sbuf_usable_end - nc.sbuf_base) // 4 - 32], f32))
        top = [0]

        def at(name, off, n, dt=f32, parts=P):
            assert off + n <= floats, (name, off + n, floats)
            return nc.alloc_sbuf_tensor_at(name, [parts, n], dt, offset=base + 4 * off)[:, :]

        def new(name, n, dt=f32):
            off = top[0]
            top[0] = off + -(-n // 8) * 8
            return at(name, off, n, dt)

        xs = new("xs", TB * D).rearrange("p (b d) -> p b d", b=TB)
        hs = new("hs", TB * D).rearrange("p (b d) -> p b d", b=TB)
        cst = new("cst", K_BAND)
        ident, tri = cst[:, K_ID:K_ID + P], cst[:, K_TRI:K_TRI + P]
        ones, iota1 = cst[:, K_ONE:K_ONE + P], cst[:, K_IOTA:K_IOTA + SLOTS]
        fold = cst[:, K_FOLD:K_FOLD + NE]
        gmix = new("gmix", D)
        gffn = new("gffn", D)
        wr = new("wr", KD * NE).rearrange("p (k e) -> p k e", k=KD)
        br = new("br", NE)
        gcol = new("gcol", KD)
        poolw = new("poolw", 4 * P).rearrange("p (g d) -> p g d", g=4)
        pscale = new("pscale", 4)
        wiT = new("wiT", SEQ)[DI:DI + NIH, :]
        wi = new("wi", TB * NIH).rearrange("p (b i) -> p b i", b=TB)
        stat = new("stat", 64)
        sq, var, std, rstd = stat[:, 0:4], stat[:, 4:6], stat[:, 6:8], stat[:, 8:10]
        lsum, linv, nlmax, warm = stat[:, 10:12], stat[:, 12:14], stat[:, 14:16], stat[:, 16:18]
        hmax, nhmax, hsum, hinv = (stat[:, 20 + 4 * i:24 + 4 * i].rearrange("p (r b) -> p r b", r=2) for i in range(4))
        m8 = stat[:, 40:48]
        keepm = new("keepm", TB * SEQ).rearrange("p (b s) -> p b s", b=TB)

        o1 = top[0]
        r1 = new("r1", 7680)
        qT = r1[:, 0:1024].rearrange("p (b t) -> p b t", b=4)
        kT = r1[:, 1024:2048].rearrange("p (b t) -> p b t", b=4)
        qiT = r1[:, 2048:2560].rearrange("p (b t) -> p b t", b=2)
        kiT = r1[:, 2560:2816]
        relu = r1[:, 2816:3840].rearrange("p (r j s) -> p r j s", r=2, j=2)
        score = r1[:, 3840:4352].rearrange("p (b s) -> p b s", b=2)
        atth = at("atth", o1 + 2048, 1024, f32r).rearrange("p (g t) -> p g t", g=4)
        attl = at("attl", o1 + 3072, 1024, f32r).rearrange("p (g t) -> p g t", g=4)
        vv = r1[:, 4352:5376].rearrange("p (b c) -> p b c", b=2)
        logit = r1[:, 5376:6144].rearrange("p (r s) -> p r s", r=2)
        prob = r1[:, 6144:6912].rearrange("p (r s) -> p r s", r=2)
        pT = r1[:, 6912:7680].rearrange("p (r s) -> p r s", r=2)
        hot = r1[0:BUCKETS, 6144:6144 + SEQ]
        table = r1[0:BUCKETS, 6400:6400 + NH]
        b1s = r1[:, 0:2048]
        b2s = r1[0:NE, 2048:3072]
        xT = r1[:, 3072:5120].rearrange("p (k t) -> p k t", k=KD)
        parts = r1[:, 5120:5376]
        gclip = r1[:, 3072:3584]
        sig = r1[:, 3584:4096]
        uclip = r1[:, 4096:4608]
        act = r1[:, 4608:5120]
        actT = r1[:, 5120:5632]
        ys = r1[:, 5632:6144]
        xgT = r1[:, 6144:6656].rearrange("p (k s) -> p k s", k=KD)
        gT = r1[:, 6656:6912]
        pick = r1[:, 6912:7040].rearrange("p (b s) -> p b s", b=TB)
        gpick = r1[:, 7040:7296].rearrange("p (b u s) -> p b u s", b=TB, u=2)
        sel = r1[:, 7296:7360]
        combT = r1[0:NE, 7360:7616]
        iota_r = r1[:, 7616:7680]
        o3 = top[0]
        r3 = new("r3", 3584)
        uu = r3[:, 0:1024].rearrange("p (b c) -> p b c", b=2)
        pooledT = r3[:, 1024:2048].rearrange("p (g t) -> p g t", g=4)
        band = r3[:, 2048:3584].rearrange("p (m t) -> p m t", t=P)
        mixh = at("mixh", o3, 1024, f32r).rearrange("p (g t) -> p g t", g=4)
        mixl = at("mixl", o3 + 2048, 1024, f32r).rearrange("p (g t) -> p g t", g=4)
        lg = r3[:, 0:80].rearrange("p (b e) -> p b e", b=2)
        lgt = r3[:, 80:160].rearrange("p (b e) -> p b e", b=2)
        top8 = r3[:, 160:176].rearrange("p (b e) -> p b e", b=2)
        rep8 = r3[:, 176:192].rearrange("p (b e) -> p b e", b=2)
        emask = r3[:, 192:256].rearrange("p (b e) -> p b e", b=2)
        eexp = r3[:, 256:320].rearrange("p (b e) -> p b e", b=2)
        comb = r3[:, 320:386].rearrange("p (b e) -> p b e", b=2)
        posn = r3[:, 386:452].rearrange("p (b e) -> p b e", b=2)
        cmax = r3[0:1, 452:453]
        count = at("count", o3 + 456, 1, i32, 1)
        o_bias = top[0]
        bias = new("bias", NH * SEQ).rearrange("p (h s) -> p h s", h=NH)
        o_ring = top[0]
        ring = new("ring", FRING * SLOT).rearrange("p (r n) -> p r n", r=FRING)
        o_gates = top[0]
        gates = new("gates", TB * 2 * D).rearrange("p (b c) -> p b c", b=TB)
        skew = at("skew", o_gates, NH * SKEW).rearrange("p (h s) -> p h s", h=NH)
        o_split = top[0]
        wh = new("wh", LOOK * PIECE, f32r).rearrange("p (i n) -> p i n", i=LOOK)
        wl = new("wl", LOOK * PIECE, f32r).rearrange("p (i n) -> p i n", i=LOOK)
        o_hT = top[0]
        hTh = new("hTh", KD * SEQ, f32r).rearrange("p (k t) -> p k t", k=KD)
        hTl = new("hTl", KD * SEQ, f32r).rearrange("p (k t) -> p k t", k=KD)
        first_front = 2 * (N_PIECES // 2 - FRING)
        e_off = [o_bias]
        e_off += [o_ring + SLOT * ((N_PIECES // 2 - FRING + i) % FRING) for i in range(FRING)]
        e_off += [o_gates, o_gates + SLOT, o_split, o_split + 2 * SLOT, o_split + SLOT, o_split + 3 * SLOT,
                  o_hT, o_hT + SLOT]
        eslot = [at(f"eslot{i}", o, SLOT) for i, o in enumerate(e_off)]

        bank = [ctx.enter_context(nc.psum_tensor(f"bank{i}", [P, HALF], f32)) for i in range(8)]
        GA, UA, GATHER, YT = bank[0:4]
        YSUM = bank[4:8]

        skew_dram = nc.dram_tensor("skew_dram", (P, NH * SKEW), f32, kind="Internal").ap()

        ring_loaded = [sem(f"ring_loaded{i}") for i in range(FRING)]
        chunk_loaded = [sem(f"chunk_loaded{i}") for i in range(ERING)]
        chunks_used = sem("chunks_used")
        high_ready, low_ready, piece_used = sem("high_ready"), sem("low_ready"), sem("piece_used")
        x_loaded = [sem(f"x_loaded{b}") for b in range(TB)]
        cst_loaded = sem("cst_loaded")
        gmix_loaded, gffn_loaded, gfin_loaded = sem("gmix_loaded"), sem("gffn_loaded"), sem("gfin_loaded")
        table_loaded, band_loaded, poolw_loaded = sem("table_loaded"), sem("band_loaded"), sem("poolw_loaded")
        router_loaded, b1_loaded, b2_loaded = sem("router_loaded"), sem("b1_loaded"), sem("b2_loaded")
        warm_ready = sem("warm_ready")
        skew_done, skew_ready = sem("skew_done"), sem("skew_ready")
        skew_saved, bias_loaded = sem("skew_saved"), sem("bias_loaded")
        squares_ready, var_ready, std_ready = sem("squares_ready"), sem("var_ready"), sem("std_ready")
        rstd_ready, h_ready = sem("rstd_ready"), sem("h_ready")
        tp_done, tp_high, tp_low, tp_evac = sem("tp_done"), sem("tp_high"), sem("tp_low"), sem("tp_evac")
        idx_ready = sem("idx_ready")
        sc_done, relu_ready, score_ready = sem("sc_done"), sem("relu_ready"), sem("score_ready")
        causal_ready, taken_ready, kept_ready = sem("causal_ready"), sem("taken_ready"), sem("kept_ready")
        keepm_ready = sem("keepm_ready")
        half_evac, gate_ready = sem("half_evac"), sem("gate_ready")
        pool_done, pool_evac, mix_high, mix_low = sem("pool_done"), sem("pool_evac"), sem("mix_high"), sem("mix_low")
        logit_done, logit_read = sem("logit_done"), sem("logit_read")
        hmax_ready, nhmax_ready, exp_ready = sem("hmax_ready"), sem("nhmax_ready"), sem("exp_ready")
        hinv_ready, prob_ready = sem("hinv_ready"), sem("prob_ready")
        pT_done, pT_ready, pv_done = sem("pT_done"), sem("pT_ready"), sem("pv_done")
        att_high, att_low = sem("att_high"), sem("att_low")
        branch_done, gated = sem("branch_done"), sem("gated")
        b1_zeroed = sem("b1_zeroed")
        wo_done, x_ready = sem("wo_done"), sem("x_ready")
        wr_ready, parts_done, parts_ready = sem("wr_ready"), sem("parts_done"), sem("parts_ready")
        router_done, routing, nlmax_ready = sem("router_done"), sem("routing"), sem("nlmax_ready")
        eexp_ready, rank_done = sem("eexp_ready"), sem("rank_done")
        combT_done, combT_ready = sem("combT_done"), sem("combT_ready")
        count_ready = sem("count_ready")
        sel_ready = sem("sel_ready")
        pick_ready, gather_done, xgT_ready = sem("pick_ready"), sem("gather_done"), sem("xgT_ready")
        gpick_ready, gT_done, gT_ready = sem("gpick_ready"), sem("gT_done"), sem("gT_ready")
        gclip_ready, sig_ready, act_ready = sem("gclip_ready"), sem("sig_ready"), sem("act_ready")
        uclip_ready, gu_ready = sem("uclip_ready"), sem("gu_ready")
        actT_done, actT_ready = sem("actT_done"), sem("actT_ready")
        y_ready, scattered = sem("y_ready"), sem("scattered")
        iota_ready = sem("iota_ready")
        out_saved = sem("out_saved")

        block = ctx.enter_context(nc.Block())

        w_in_k = w_in.rearrange("(k p) n -> p k n", p=P)
        w1_k = w1.rearrange("e (k p) n -> e p k n", p=P)
        w2_k = w2.rearrange("e (k p) n -> e p k n", p=P)

        def piece_cols(t, n):
            v = t.rearrange("p (k n) -> p k n", k=2)
            return v[:, :, 0:N_IDX] if n < P_Q else v

        def ring_piece(n):
            return piece_cols(ring[:, (n // 2) % FRING, (n % 2) * PIECE:(n % 2 + 1) * PIECE], n)

        @block.sync
        def _(sp):
            for b in range(TB):
                sp.dma_start(xs[:, b, :], x[b * P:(b + 1) * P, :]).then_inc(x_loaded[b], 16)

            def load(use, src, k, n):
                if use >= FRING:
                    sp.wait_ge(low_ready, 2 * (use - FRING) + 2)
                dst = ring[:, use % FRING, :].rearrange("p (k n) -> p k n", k=k)[:, :, 0:n]
                sp.dma_start(dst, src).then_inc(ring_loaded[use % FRING], 16)

            use = 0
            for c0, n in ((C_QI, N_IDX), (C_Q, 512), (C_K, 512), (C_V, 512), (C_POOL, 512),
                          *((C_GATE + 512 * i, 512) for i in range(4))):
                for i in range(2):
                    load(use, w_in_k[:, 4 * i:4 * i + 4, c0:c0 + n], 4, n)
                    use += 1
            for w in (w_bp, w_ba, w_out):
                wk = w.rearrange("(k p) n -> p k n", p=P)
                for i in range(wk.shape[1] // 2):
                    load(use, wk[:, 2 * i:2 * i + 2, :], 2, D)
                    use += 1

            def chunk(e, j, s):
                if j < KD:
                    dst, src = eslot[s], w1_k[e, :, j, :]
                else:
                    dst = eslot[s].rearrange("p (k n) -> p k n", k=2)
                    src = w2_k[e, :, 2 * (j - KD):2 * (j - KD) + 2, :]
                sp.dma_start(dst, src).then_inc(chunk_loaded[s], 16)

            for c in range(GROUP * CHUNKS):
                if c == 0:
                    sp.wait_ge(logit_read, NH)
                elif c <= FRING:
                    sp.wait_ge(low_ready, first_front + 2 * c)
                elif c in (8, 9):
                    sp.wait_ge(gated, 12)
                elif c in (10, 11):
                    sp.wait_ge(piece_used, N_PIECES - 2)
                elif c in (12, 13, 14, 15):
                    sp.wait_ge(piece_used, N_PIECES)
                else:
                    sp.wait_ge(chunks_used, c - ERING + 1)
                chunk(c // CHUNKS, c % CHUNKS, c % ERING)

            def load_group(r, g):
                for c in range(GROUP * CHUNKS):
                    sp.wait_ge(chunks_used, (r * NE + g * GROUP) * CHUNKS + c - ERING + 1)
                    chunk(g * GROUP + c // CHUNKS, c % CHUNKS, c % ERING)

            with sp.Fori(1, NE // GROUP) as g:
                load_group(0, g)
            sp.wait_ge(count_ready, 1)
            most = sp.value_load(count[0:1, 0:1], min_val=0, max_val=SEQ)
            with sp.If(most > SLOTS):
                with sp.Fori(1, ROUNDS) as r:
                    with sp.Fori(0, NE // GROUP) as g:
                        load_group(r, g)
            for q in range(4):
                b, half = q // 2, slice(q % 2 * HALF, (q % 2 + 1) * HALF)
                sp.wait_ge(h_ready, 2 * TB + q + 1)
                sp.dma_start(out[b * P:(b + 1) * P, half], hs[:, b, half]).then_inc(out_saved, 16)
            sp.wait_ge(out_saved, 16 * 4)

        @block.gpsimd
        def _(pool):
            nc.gpsimd.memset(warm, 1.0).then_inc(warm_ready, 1)
            nc.gpsimd.memset(skew[:, :, SEQ:SKEW], 0.0).then_inc(warm_ready, 1)
            pool.wait_ge(skew_ready, 4)
            pool.wait_ge(warm_ready, 2)
            pool.dma_start(skew_dram, skew.rearrange("p h s -> p (h s)")).then_inc(skew_saved, 16)
            pool.wait_ge(skew_saved, 16)
            skewed = bass.AP(tensor=skew_dram.tensor, offset=P - 1, ap=[[NH * SKEW - 1, P], [SKEW, NH], [1, SEQ]])
            pool.dma_start(bias, skewed).then_inc(bias_loaded, 16)
            for b in range(TB):
                n = P * (b + 1)
                pool.wait_ge(score_ready, b + 1)
                nc.gpsimd.affine_select(out=score[:, b, 0:n], in_=score[:, b, 0:n], compare_op=ALU.is_ge,
                                        fill=MASKED, base=P * b, pattern=[[-1, n]],
                                        channel_multiplier=1).then_inc(causal_ready, 1)
            for b in range(TB):
                n = P * (b + 1)
                pool.wait_ge(kept_ready, b + 1)
                nc.gpsimd.affine_select(out=keepm[:, b, 0:n], in_=keepm[:, b, 0:n], compare_op=ALU.is_ge,
                                        fill=NEG_BIG, base=P * b, pattern=[[-1, n]],
                                        channel_multiplier=1).then_inc(keepm_ready, 1)
            pool.wait_ge(h_ready, TB)
            pool.dma_start(gmix, final_norm.partition_broadcast(P)).then_inc(gfin_loaded, 16)
            pool.wait_ge(logit_done, NH)
            nc.gpsimd.memset(b1s, 0.0).then_inc(b1_zeroed, 1)
            pool.wait_ge(b1_zeroed, 1)
            pool.dma_start(b1s[0:NE, :], b1).then_inc(b1_loaded, 16)
            pool.wait_ge(piece_used, P_WO)
            pool.dma_start(b2s, b2).then_inc(b2_loaded, 16)

        @block.scalar
        def _(a):
            a.dma_start(gmix, mix_norm.partition_broadcast(P)).then_inc(gmix_loaded, 16)
            a.dma_start(hot, bucket_hot).then_inc(table_loaded, 16)
            a.dma_start(table, rel_bias).then_inc(table_loaded, 16)
            a.dma_start(cst, consts[:, 0:K_BAND]).then_inc(cst_loaded, 16)
            a.dma_start(band, consts[:, K_BAND:].rearrange("p (m t) -> p m t", t=P)).then_inc(band_loaded, 16)
            a.dma_start(poolw, pool_w.rearrange("g c d -> c g d")).then_inc(poolw_loaded, 16)
            a.dma_start(pscale, pool_scale).then_inc(poolw_loaded, 16)
            a.dma_start(gffn, ffn_norm.partition_broadcast(P)).then_inc(gffn_loaded, 16)
            a.dma_start(wr, w_router.rearrange("(k p) e -> p k e", p=P)).then_inc(router_loaded, 16)
            a.dma_start(br, b_router.partition_broadcast(P)).then_inc(router_loaded, 16)
            a.dma_start(gcol, ffn_cols).then_inc(router_loaded, 16)

            def squares(i, order):
                for n, q in enumerate(order):
                    b, c = q // 2, q % 2
                    half = slice(c * HALF, (c + 1) * HALF)
                    if i == 0:
                        a.wait_ge(x_loaded[b], 16)
                    elif i == 1:
                        a.wait_ge(x_ready, n + 1)
                    elif n == 2:
                        a.wait_ge(scattered, 2 * NE)
                    nc.scalar.activation(hs[:, b, half], YSUM[q][:, :] if i == 2 else xs[:, b, half], ACT.Square,
                                         accum_out=sq[:, q:q + 1]).then_inc(squares_ready, 1)
                    if i == 2 and n % 2:
                        root(i, b)
                if i < 2:
                    for b in range(TB):
                        root(i, b)

            def root(i, b):
                a.wait_ge(var_ready, 2 * i + b + 1)
                nc.scalar.activation(std[:, b:b + 1], var[:, b:b + 1], ACT.Sqrt, scale=1.0 / D).then_inc(std_ready, 1)

            def fetch_root_table():
                nc.scalar.activation(warm[:, 0:1], warm[:, 1:2], ACT.Sqrt)

            def high(n):
                use = n // 2
                a.wait_ge(ring_loaded[use % FRING], 16 * (use // FRING + 1))
                if n >= LOOK:
                    a.wait_ge(piece_used, n - LOOK + 1)
                nc.scalar.activation(piece_cols(wh[:, n % LOOK, :], n), ring_piece(n), ACT.Copy).then_inc(high_ready, 1)

            def transposed_high(i, banks=(0, 1, 2, 3)):
                for j in banks:
                    a.wait_ge(tp_done, 4 * i + j + 1)
                    nc.scalar.activation(hTh[:, 2 * j:2 * j + 2, :],
                                         bank[j][:, :].rearrange("p (k t) -> p k t", k=2), ACT.Copy).then_inc(tp_high, 1)

            def indexer_operands():
                a.wait_ge(piece_used, P_Q)
                for half in (slice(0, DI), slice(DI, 2 * DI)):
                    nc.scalar.activation(kiT[half, :], bank[5][0:DI, 0:SEQ], ACT.Copy).then_inc(idx_ready, 1)
                nc.scalar.activation(wiT, bank[5][DI:DI + NIH, 0:SEQ], ACT.Copy).then_inc(idx_ready, 1)
                nc.scalar.activation(qiT, bank[4][:, :].rearrange("p (b t) -> p b t", b=2), ACT.Copy)\
                    .then_inc(idx_ready, 1)

            def indexer_relu():
                for b in range(TB):
                    n = P * (b + 1)
                    a.wait_ge(sc_done, b + 1)
                    if b == 0:
                        nc.scalar.activation(wi, bank[5][:, 3 * P:3 * P + TB * NIH].rearrange("p (b i) -> p b i", b=TB),
                                             ACT.Copy).then_inc(idx_ready, 1)
                    else:
                        a.wait_ge(score_ready, 1)
                    for r in range(2):
                        src = bank[4 + 2 * b + r][:, :].rearrange("p (j s) -> p j s", j=2)[:, :, 0:n]
                        nc.scalar.activation(relu[:, r, :, 0:n], src, ACT.Relu,
                                             scale=float(DI ** -0.5 * NIH ** -0.5)).then_inc(relu_ready, 1)

            def group_out(g):
                a.wait_ge(piece_used, P_Q + 4 * (g + 1))
                for b in range(2):
                    src = bank[2 * (g % 2) + b][:, :]
                    pair = src.rearrange("p (b t) -> p b t", b=2)
                    if g < 2:
                        nc.scalar.activation((qT if g == 0 else kT)[:, 2 * b:2 * b + 2, :], pair, ACT.Copy)\
                            .then_inc(half_evac, 1)
                    elif g < 4:
                        nc.scalar.activation((vv if g == 2 else uu)[:, b, :], src, ACT.Copy).then_inc(half_evac, 1)
                    else:
                        if g == 4:
                            a.wait_ge(bias_loaded, 16)
                        nc.scalar.activation(gates[:, b, HALF * (g - 4):HALF * (g - 3)], src, ACT.Copy)\
                            .then_inc(half_evac, 1)

            def pooled():
                for i in range(2):
                    a.wait_ge(pool_done, i + 1)
                    nc.scalar.activation(pooledT[:, 2 * i:2 * i + 2, :],
                                         bank[4 + i][:, :].rearrange("p (g t) -> p g t", g=2), ACT.Copy)\
                        .then_inc(pool_evac, 1)

            def mixed_high():
                a.wait_ge(poolw_loaded, 32)
                for g in range(4):
                    a.wait_ge(pool_done, 2 + g // 2 + 1)
                    nc.scalar.activation(mixh[:, g, :], bank[4 + g // 2][:, (g % 2) * SEQ:(g % 2 + 1) * SEQ], ACT.Copy,
                                         scale=pscale[:, g:g + 1]).then_inc(mix_high, 1)

            def exps(h):
                r = h % 2
                a.wait_ge(nhmax_ready, h + 1)
                if h >= 2:
                    a.wait_ge(pT_done, h - 1)
                for b, (s0, n) in enumerate(((0, P), (P, SEQ))):
                    nc.scalar.activation(prob[:, r, s0:s0 + n], logit[:, r, s0:s0 + n], ACT.Exp,
                                         bias=nhmax[:, r, b:b + 1], accum_out=hsum[:, r, b:b + 1])\
                        .then_inc(exp_ready, 1)

            def probs_transposed(h):
                a.wait_ge(pT_done, h + 1)
                if h >= 2:
                    a.wait_ge(pv_done, h - 1)
                nc.scalar.activation(pT[:, h % 2, :], bank[4][:, 0:384], ACT.Copy).then_inc(pT_ready, 1)

            def attended_high(pr):
                a.wait_ge(pv_done, 2 * pr + 2)
                nc.scalar.activation(atth[:, pr, :], bank[5][:, 0:SEQ], ACT.Copy).then_inc(att_high, 1)

            a.wait_ge(warm_ready, 1)
            fetch_root_table()
            squares(0, range(4))
            for i in (0, 2):
                a.wait_ge(skew_done, i // 2 + 1)
                nc.scalar.activation(skew[:, 2 * i:2 * i + 2, 0:SEQ], bank[4 + i][:, :].rearrange("p (h s) -> p h s", h=2),
                                     ACT.Copy).then_inc(skew_ready, 1)
            for n in range(N_PIECES):
                high(n)
                if n == 1:
                    transposed_high(0)
                elif n == P_Q + 3:
                    indexer_operands()
                elif n == P_Q + 4:
                    indexer_relu()
                elif n in (11, 15, 19, 23, 31, 35):
                    group_out((n - 11) // 4)
                elif n == 25:
                    pooled()
                elif n == 27:
                    mixed_high()
                    group_out(4)
                elif n == 39:
                    group_out(7)
                elif n in (47, 48):
                    transposed_high(1, (0, 1) if n == 47 else (2, 3))
                q, p = n % 4, n // 4
                if 24 <= n < 40 and q in (0, 1):
                    exps(2 * (p - 6) + q)
                if 28 <= n < 44:
                    if q in (0, 1):
                        probs_transposed(2 * (p - 7) + q)
                    elif q == 2:
                        attended_high(p - 7)
                if n in (39, 41):
                    c = D * ((n - 39) // 2)
                    a.wait_ge(half_evac, 16)
                    for b in range(TB):
                        nc.scalar.activation(gates[:, b, c:c + D], gates[:, b, c:c + D], ACT.Sigmoid)\
                            .then_inc(gate_ready, 1)
            fetch_root_table()
            squares(1, ORDER)
            for j in (2, 3):
                a.wait_ge(tp_done, 8 + j + 1)
                nc.scalar.activation(xT[:, 2 * j:2 * j + 2, :],
                                     bank[j][:, :].rearrange("p (k t) -> p k t", k=2), ACT.Copy).then_inc(tp_evac, 1)
            a.wait_ge(parts_done, 1)
            nc.scalar.activation(parts, bank[2][:, 0:SEQ], ACT.Copy).then_inc(parts_ready, 1)
            a.wait_ge(nlmax_ready, 1)
            for b in range(TB):
                nc.scalar.activation(eexp[:, b, :], lg[:, b, 0:NE], ACT.Exp, bias=nlmax[:, b:b + 1])\
                    .then_inc(eexp_ready, 1)
            a.wait_ge(combT_done, 1)
            nc.scalar.activation(combT, bank[3][0:NE, 0:SEQ], ACT.Copy).then_inc(combT_ready, 1)

            def copy_xgT(gathers):
                a.wait_ge(gather_done, gathers)
                nc.scalar.activation(xgT, GATHER[:, :].rearrange("p (k s) -> p k s", k=KD), ACT.Copy)\
                    .then_inc(xgT_ready, 1)

            def experts_round(r):
                copy_xgT(r * (NE + 1) + 1)
                with a.Fori(0, NE // GROUP) as g:
                    for i in range(GROUP):
                        u = r * NE + g * GROUP + i
                        a.wait_ge(gclip_ready, u + 1)
                        nc.scalar.activation(sig, gclip, ACT.Sigmoid, scale=ALPHA).then_inc(sig_ready, 1)
                        a.wait_ge(gT_done, u + 1)
                        nc.scalar.activation(gT, YT[:, 0:SEQ], ACT.Copy).then_inc(gT_ready, 1)
                        copy_xgT(r * (NE + 1) + g * GROUP + i + 2)
                        a.wait_ge(actT_done, u + 1)
                        nc.scalar.activation(actT, GA[:, :], ACT.Copy).then_inc(actT_ready, 1)
                        a.wait_ge(chunks_used, u * CHUNKS + CHUNKS)
                        nc.scalar.activation(ys, YT[:, :], ACT.Copy).then_inc(y_ready, 1)

            experts_round(0)
            a.wait_ge(count_ready, 1)
            most = a.value_load(count[0:1, 0:1], min_val=0, max_val=SEQ)
            with a.If(most > SLOTS):
                with a.Fori(1, ROUNDS) as r:
                    experts_round(r)
                a.wait_ge(scattered, ROUNDS * 2 * NE)
            fetch_root_table()
            a.wait_ge(scattered, 2 * NE - 1)
            squares(2, range(4))

        @block.vector
        def _(v):
            def inverse_root(i, b, squares_needed):
                v.wait_ge(squares_ready, 4 * i + squares_needed)
                nc.vector.tensor_scalar(var[:, b:b + 1], sq[:, 2 * b:2 * b + 1], sq[:, 2 * b + 1:2 * b + 2], D * EPS,
                                        ALU.add, ALU.add).then_inc(var_ready, 1)

            def scaled(i, b):
                v.wait_ge(std_ready, 2 * i + b + 1)
                nc.vector.reciprocal(rstd[:, b:b + 1], std[:, b:b + 1]).then_inc(rstd_ready, 1)
                v.wait_ge(rstd_ready, 2 * i + b + 1)
                v.wait_ge(*((gmix_loaded, 16), (gffn_loaded, 16), (gfin_loaded, 16))[i])
                gain = gffn if i == 1 else gmix
                if i < 2:
                    nc.vector.scalar_tensor_tensor(out=hs[:, b, :], in0=xs[:, b, :], scalar=rstd[:, b:b + 1],
                                                   in1=gain, op0=ALU.mult, op1=ALU.mult).then_inc(h_ready, 1)
                else:
                    for c in range(2):
                        half = slice(c * HALF, (c + 1) * HALF)
                        nc.vector.scalar_tensor_tensor(out=hs[:, b, half], in0=YSUM[2 * b + c][:, :],
                                                       scalar=rstd[:, b:b + 1], in1=gain[:, half],
                                                       op0=ALU.mult, op1=ALU.mult).then_inc(h_ready, 1)

            def low(n):
                v.wait_ge(high_ready, n + 1)
                nc.vector.tensor_tensor(piece_cols(wl[:, n % LOOK, :], n), ring_piece(n),
                                        piece_cols(wh[:, n % LOOK, :], n).bitcast(f32), ALU.subtract)\
                    .then_inc(low_ready, 1)

            def transposed_low(i, banks=(0, 1, 2, 3)):
                for j in banks:
                    v.wait_ge(tp_high, 4 * i + j + 1)
                    k = slice(2 * j, 2 * j + 2)
                    nc.vector.tensor_tensor(hTl[:, k, :], bank[j][:, :].rearrange("p (k t) -> p k t", k=2),
                                            hTh[:, k, :].bitcast(f32), ALU.subtract).then_inc(tp_low, 1)

            steps = [0]

            def taking(ins):
                ins.then_inc(taken_ready, 1)
                steps[0] += 1
                v.wait_ge(taken_ready, steps[0])

            def scores():
                for b in range(TB):
                    n = P * (b + 1)
                    v.wait_ge(idx_ready, 5)
                    v.wait_ge(relu_ready, 2 * b + 2)
                    for i in range(NIH):
                        rl, w = relu[:, i % 2, i // 2, 0:n], wi[:, b, i:i + 1]
                        if i == 0:
                            ins = nc.vector.tensor_scalar(score[:, b, 0:n], rl, w, None, ALU.mult)
                        else:
                            ins = nc.vector.scalar_tensor_tensor(out=score[:, b, 0:n], in0=rl, scalar=w,
                                                                 in1=score[:, b, 0:n], op0=ALU.mult, op1=ALU.add)
                        if i < NIH - 1:
                            taking(ins)
                    ins.then_inc(score_ready, 1)

            def take16(b, last):
                n = P * (b + 1)
                v.wait_ge(causal_ready, b + 1)
                for _ in range(2):
                    taking(nc.vector.max(m8, score[:, b, 0:n]))
                    taking(nc.vector.match_replace(score[:, b, 0:n], m8, score[:, b, 0:n], TAKEN))
                if last:
                    nc.vector.tensor_scalar(keepm[:, b, 0:n], score[:, b, 0:n], (MASKED + TAKEN) / 2, NEG_BIG,
                                            ALU.is_ge, ALU.mult).then_inc(kept_ready, 1)

            def mixed_low():
                for g in range(4):
                    v.wait_ge(mix_high, g // 2 * 2 + 2)
                    nc.vector.scalar_tensor_tensor(out=mixl[:, g, :], in0=bank[4 + g // 2][:, (g % 2) * SEQ:(g % 2 + 1) * SEQ],
                                                   scalar=pscale[:, g:g + 1], in1=mixh[:, g, :].bitcast(f32),
                                                   op0=ALU.mult, op1=ALU.subtract).then_inc(mix_low, 1)

            def softmax_in(h):
                r = h % 2
                lb = bank[6 + r]
                v.wait_ge(logit_done, h + 1)
                if h == 0:
                    v.wait_ge(bias_loaded, 16)
                    v.wait_ge(keepm_ready, 2)
                if h >= 2:
                    v.wait_ge(exp_ready, 2 * (h - 1))
                for s0, n, c0 in ((0, P, P), (P, SEQ, 0)):
                    ins = nc.vector.scalar_tensor_tensor(out=logit[:, r, s0:s0 + n], in0=lb[:, s0:s0 + n],
                                                         scalar=float(DH ** -0.5), in1=bias[:, h, c0:c0 + n],
                                                         op0=ALU.mult, op1=ALU.add)
                ins.then_inc(logit_read, 1)
                v.wait_ge(logit_read, h + 1)
                for b, (s0, n) in enumerate(((0, P), (P, SEQ))):
                    nc.vector.tensor_tensor_reduce(out=logit[:, r, s0:s0 + n], in0=logit[:, r, s0:s0 + n],
                                                   in1=keepm[:, b, 0:n], scale=1.0, scalar=-3.4e38,
                                                   op0=ALU.add, op1=ALU.max, accum_out=hmax[:, r, b:b + 1])\
                        .then_inc(hmax_ready, 1)
                v.wait_ge(hmax_ready, 2 * h + 2)
                nc.vector.tensor_scalar(nhmax[:, r, :], hmax[:, r, :], -1.0, None, ALU.mult).then_inc(nhmax_ready, 1)

            def softmax_out(h):
                r = h % 2
                v.wait_ge(exp_ready, 2 * h + 2)
                nc.vector.reciprocal(hinv[:, r, :], hsum[:, r, :]).then_inc(hinv_ready, 1)
                v.wait_ge(hinv_ready, h + 1)
                for b, (s0, n) in enumerate(((0, P), (P, SEQ))):
                    ins = nc.vector.tensor_scalar(prob[:, r, s0:s0 + n], prob[:, r, s0:s0 + n],
                                                  hinv[:, r, b:b + 1], None, ALU.mult)
                ins.then_inc(prob_ready, 1)

            def attended_low(pr):
                v.wait_ge(att_high, pr + 1)
                nc.vector.tensor_tensor(attl[:, pr, :], bank[5][:, 0:SEQ], atth[:, pr, :].bitcast(f32), ALU.subtract)\
                    .then_inc(att_low, 1)

            def gate_quarter(i, n):
                q = ORDER[n] if i else n
                b, c = q // 2, q % 2
                if n < 3:
                    v.wait_ge(branch_done, 3 * i + n + 1)
                else:
                    v.wait_ge(piece_used, (P_BA, P_WO)[i])
                v.wait_ge(gate_ready, 2 * i + b + 1)
                g = gates[:, b, D * i + HALF * c:D * i + HALF * (c + 1)]
                m = hs[:, b, HALF * c:HALF * (c + 1)]
                nc.vector.tensor_tensor(g if i else m, bank[4 * i + q][:, :], g, ALU.mult).then_inc(gated, 1)
                if i:
                    v.wait_ge(gated, 4 + 2 * n + 1)
                    nc.vector.tensor_tensor(m, m, g, ALU.add).then_inc(gated, 1)

            for b in range(TB):
                v.wait_ge(x_loaded[b], 16)
                inverse_root(0, b, 2 * b + 2)
            for b in range(TB):
                scaled(0, b)
            for i in (1, 3):
                v.wait_ge(skew_done, i // 2 + 1)
                nc.vector.tensor_copy(skew[:, 2 * i:2 * i + 2, 0:SEQ], bank[4 + i][:, :].rearrange("p (h s) -> p h s", h=2))\
                    .then_inc(skew_ready, 1)
            for n in range(N_PIECES):
                low(n)
                if n == 1:
                    transposed_low(0)
                elif n == P_Q + 4:
                    scores()
                elif P_K < n <= P_K + 8:
                    take16((n - P_K - 1) // 4, n % 4 == 0)
                elif n == 27:
                    mixed_low()
                elif n == 48:
                    transposed_low(1, (2, 3))
                q, p = n % 4, n // 4
                if 23 <= n < 37:
                    if q == 3:
                        softmax_in(2 * (p - 5))
                    elif q == 0:
                        softmax_in(2 * (p - 6) + 1)
                if 25 <= n < 39 and q in (1, 2):
                    softmax_out(2 * (p - 6) + q - 1)
                if 30 <= n < 43 and q == 2:
                    attended_low(p - 7)
                if n == 43:
                    for i in range(4):
                        gate_quarter(0, i)
                elif n == 46:
                    for i in range(3):
                        gate_quarter(1, i)
                    transposed_low(1, (0, 1))
                    gate_quarter(1, 3)
            nc.vector.memset(lg[:, :, NE:], MASKED)
            nc.vector.memset(posn, 0.0)
            nc.vector.memset(comb, 0.0)
            nc.vector.memset(rep8, MASKED)
            nc.vector.tensor_copy(iota_r, iota1).then_inc(iota_ready, 1)

            def make_sel(e):
                nc.vector.tensor_copy(sel, ident[:, bass.ds(e, 1)].to_broadcast([P, SLOTS])).then_inc(sel_ready, 1)

            v.wait_ge(router_loaded, 48)
            nc.vector.tensor_tensor(wr, wr, gcol.unsqueeze(2).to_broadcast([P, KD, NE]), ALU.mult).then_inc(wr_ready, 1)
            make_sel(0)
            for n, q in enumerate(ORDER):
                if n < 3:
                    v.wait_ge(wo_done, n + 1)
                else:
                    v.wait_ge(piece_used, N_PIECES)
                xh = xs[:, q // 2, HALF * (q % 2):HALF * (q % 2 + 1)]
                nc.vector.tensor_tensor(xh, bank[4 + q][:, :], xh, ALU.add).then_inc(x_ready, 1)
            for j in (0, 1):
                v.wait_ge(tp_done, 8 + j + 1)
                nc.vector.tensor_copy(xT[:, 2 * j:2 * j + 2, :],
                                      bank[j][:, :].rearrange("p (k t) -> p k t", k=2)).then_inc(tp_evac, 1)
            for b in range(TB):
                inverse_root(1, b, 3 + b)
            for b in range(TB):
                scaled(1, b)
            v.wait_ge(iota_ready, 1)
            v.wait_ge(router_done, 1)
            routed = [0]

            def link(ins):
                ins.then_inc(routing, 1)
                routed[0] += 1
                v.wait_ge(routing, routed[0])

            for b in range(TB):
                ins = nc.vector.scalar_tensor_tensor(out=lg[:, b, 0:NE], in0=bank[3][:, b * NE:(b + 1) * NE],
                                                     scalar=rstd[:, b:b + 1], in1=br, op0=ALU.mult, op1=ALU.add)
            link(ins)
            for b in range(TB):
                ins = nc.vector.max(top8[:, b, :], lg[:, b, 0:NE])
            link(ins)
            nc.vector.tensor_scalar(nlmax, top8[:, :, 0], -1.0, None, ALU.mult).then_inc(nlmax_ready, 1)
            link(nc.vector.tensor_copy(rep8[:, :, 0:TOPE], top8[:, :, 0:TOPE]))
            for b in range(TB):
                ins = nc.vector.match_replace(lgt[:, b, :], rep8[:, b, :], lg[:, b, :], TAKEN)
            link(ins)
            link(nc.vector.tensor_scalar(emask, lgt[:, :, 0:NE], (MASKED + TAKEN) / 2, None, ALU.is_lt))
            assert routed[0] == R_MASK
            v.wait_ge(eexp_ready, 2)
            link(nc.vector.tensor_tensor(eexp, eexp, emask, ALU.mult))
            link(nc.vector.tensor_reduce(lsum, eexp, X, ALU.add))
            link(nc.vector.reciprocal(linv, lsum))
            for b in range(TB):
                ins = nc.vector.tensor_scalar(comb[:, b, 0:NE], eexp[:, b, :], linv[:, b:b + 1], None, ALU.mult)
            link(ins)
            assert routed[0] == R_COMB
            v.wait_ge(rank_done, 1)
            link(nc.vector.scalar_tensor_tensor(out=posn[:, :, 0:NE],
                                                in0=bank[2][:, 0:2 * NE].rearrange("p (b e) -> p b e", b=2),
                                                scalar=1.0, in1=emask, op0=ALU.add, op1=ALU.mult))
            link(nc.vector.tensor_reduce(cmax, bank[2][0:1, 2 * NE:3 * NE], X, ALU.max))
            assert routed[0] == R_COUNT

            def make_pick(e):
                for b in range(TB):
                    ins = nc.vector.tensor_scalar(pick[:, b, :], iota_r, posn[:, b, bass.ds(e, 1)], None, ALU.is_equal)
                ins.then_inc(pick_ready, 1)

            def experts_round(r):
                if not isinstance(r, int):
                    v.wait_ge(scattered, r * (2 * NE))
                    nc.vector.tensor_scalar(iota_r, iota_r, float(SLOTS), None, ALU.add).then_inc(iota_ready, 1)
                    v.wait_ge(iota_ready, r + 1)
                make_pick(0)
                if not isinstance(r, int):
                    make_sel(0)
                else:
                    nc.vector.tensor_copy(count, cmax).then_inc(count_ready, 1)
                with v.Fori(0, NE // GROUP) as g:
                    for i in range(GROUP):
                        e = g * GROUP + i
                        u = r * NE + e
                        v.wait_ge(gather_done, r * (NE + 1) + e + 1)
                        for b in range(TB):
                            ins = nc.vector.tensor_scalar(gpick[:, b, :, :], iota_r.unsqueeze(1).to_broadcast([P, 2, SLOTS]),
                                                          posn[:, b, bass.ds(e, 1)], comb[:, b, bass.ds(e, 1)],
                                                          ALU.is_equal, ALU.mult)
                        ins.then_inc(gpick_ready, 1)
                        make_pick(e + 1)
                        v.wait_ge(chunks_used, u * CHUNKS + KD)
                        nc.vector.tensor_scalar(gclip, GA[:, :], LIMIT, None, ALU.min).then_inc(gclip_ready, 1)
                        nc.vector.tensor_scalar(uclip, UA[:, :], LIMIT, -LIMIT, ALU.min, ALU.max).then_inc(uclip_ready, 1)
                        v.wait_ge(uclip_ready, u + 1)
                        nc.vector.scalar_tensor_tensor(out=uclip, in0=uclip, scalar=1.0, in1=gclip,
                                                       op0=ALU.add, op1=ALU.mult).then_inc(gu_ready, 1)
                        v.wait_ge(sig_ready, u + 1)
                        v.wait_ge(gu_ready, u + 1)
                        nc.vector.tensor_tensor(act, uclip, sig, ALU.mult).then_inc(act_ready, 1)
                        make_sel(e + 1)

            experts_round(0)
            v.wait_ge(count_ready, 1)
            most = v.value_load(count[0:1, 0:1], min_val=0, max_val=SEQ)
            with v.If(most > SLOTS):
                with v.Fori(1, ROUNDS) as r:
                    experts_round(r)
            for b in range(TB):
                inverse_root(2, b, 2 * b + 2)
                scaled(2, b)

        @block.tensor
        def _(pe):
            mm = nc.tensor.matmul

            pe.wait_ge(table_loaded, 32)
            for h in range(NH):
                ins = mm(bank[4 + h // 2][:, (h % 2) * SEQ:(h % 2 + 1) * SEQ], table[:, h:h + 1].to_broadcast([BUCKETS, P]),
                         hot, start=True, stop=True)
                if h % 4 == 3:
                    ins.then_inc(skew_done, 1)

            def transposes(src, columns, ready):
                for c in columns:
                    for b in range(TB):
                        pe.wait_ge(*ready(b, c))
                        for j in (2 * c, 2 * c + 1):
                            for k in (2 * j, 2 * j + 1):
                                o = (k % 2) * SEQ + b * P
                                ins = nc.tensor.transpose(bank[j][:, o:o + P], src[:, b, k * P:(k + 1) * P], ident)
                            if b == TB - 1:
                                ins.then_inc(tp_done, 1)

            def tok(t, k, b):
                return t[:, k, b * P:(b + 1) * P]

            def three(o, ah, al, bh, bl, start, stop, first_in_bank=True):
                mm(o, ah, bh, start=start and first_in_bank, stop=False, skip_group_check=True)
                mm(o, ah, bl, start=False, stop=False, skip_group_check=True)
                return mm(o, al, bh, start=False, stop=stop, skip_group_check=True)

            def piece_idx(n):
                h, l = piece_cols(wh[:, n % LOOK, :], n), piece_cols(wl[:, n % LOOK, :], n)
                for i in range(2):
                    k = 2 * n + i
                    for blk, (bk, c0) in enumerate(((bank[4], 0), (bank[4], SEQ), (bank[5], 0))):
                        c = slice(blk * P, (blk + 1) * P)
                        ins = three(bk[:, c0:c0 + SEQ], h[:, i, c], l[:, i, c], hTh[:, k, :], hTl[:, k, :],
                                    k == 0, k == KD - 1, c0 == 0)
                ins.then_inc(piece_used, 1)

            def piece_group(n):
                g, kp = (n - P_Q) // 4, (n - P_Q) % 4
                h, l = piece_cols(wh[:, n % LOOK, :], n), piece_cols(wl[:, n % LOOK, :], n)
                if g >= 2 and kp == 0:
                    pe.wait_ge(half_evac, 2 * (g - 1))
                for i in range(2):
                    k = 2 * kp + i
                    st, sp_ = k == 0, k == KD - 1
                    if g < 2:
                        for blk in range(4):
                            c = slice(blk * P, (blk + 1) * P)
                            ins = three(bank[2 * (g % 2) + blk // 2][:, (blk % 2) * SEQ:(blk % 2 + 1) * SEQ],
                                        h[:, i, c], l[:, i, c], hTh[:, k, :], hTl[:, k, :], st, sp_, blk % 2 == 0)
                    else:
                        for b in range(TB):
                            ins = three(bank[2 * (g % 2) + b][:, :], tok(hTh, k, b), tok(hTl, k, b),
                                        h[:, i, :], l[:, i, :], st, sp_)
                ins.then_inc(piece_used, 1)

            def piece_product(n, n0, nk, ah, al, banks, done, order):
                k = n - n0
                h, l = wh[:, n % LOOK, :], wl[:, n % LOOK, :]
                for i, q in enumerate(order):
                    if n == P_BP:
                        pe.wait_ge(half_evac, 14 if q < 2 else 16)
                    if n == P_WO:
                        pe.wait_ge(gated, 4 + 2 * i + 1)
                    b, c = q // 2, slice((q % 2) * HALF, (q % 2 + 1) * HALF)
                    ins = three(banks[q][:, :], tok(ah, k, b), tok(al, k, b), h[:, c], l[:, c], k == 0, k == nk - 1)
                    if k == nk - 1 and i < 3:
                        ins.then_inc(done, 1)
                ins.then_inc(piece_used, 1)

            def indexer_scores():
                pe.wait_ge(idx_ready, 4)
                for b in range(TB):
                    nc.tensor.transpose(bank[5][:, 3 * P + NIH * b:3 * P + NIH * (b + 1)], wiT[:, b * P:(b + 1) * P],
                                        ident[DI:DI + NIH, DI:DI + NIH])
                for b in range(TB):
                    for i in range(NIH):
                        r, c = DI * (i % 2), SEQ * (i // 2)
                        ins = mm(bank[4 + 2 * b + i % 2][:, c:c + P * (b + 1)], qiT[r:r + DI, i // 2, b * P:(b + 1) * P],
                                 kiT[r:r + DI, 0:P * (b + 1)], start=True, stop=True)
                    ins.then_inc(sc_done, 1)

            def pooling():
                pe.wait_ge(half_evac, 8)
                pe.wait_ge(band_loaded, 16)
                pe.wait_ge(relu_ready, 4)
                for g in range(4):
                    ug, bk, c = slice(g * P, (g + 1) * P), bank[4 + g // 2], (g % 2) * SEQ
                    mm(bk[:, c:c + P], uu[:, 0, ug], band[:, 3 * g, :], start=True, stop=True)
                    mm(bk[:, c + P:c + SEQ], uu[:, 0, ug], band[:, 3 * g + 1, :], start=True, stop=False)
                    ins = mm(bk[:, c + P:c + SEQ], uu[:, 1, ug], band[:, 3 * g + 2, :], start=False, stop=True)
                    if g % 2:
                        ins.then_inc(pool_done, 1)

            def mixing():
                pe.wait_ge(poolw_loaded, 32)
                for g in range(4):
                    pe.wait_ge(pool_evac, 1 + g // 2)
                    ins = mm(bank[4 + g // 2][:, (g % 2) * SEQ:(g % 2 + 1) * SEQ], poolw[:, g, :], pooledT[:, g, :],
                             start=True, stop=True)
                    if g % 2:
                        ins.then_inc(pool_done, 1)

            def logits(p):
                if p == 0:
                    pe.wait_ge(half_evac, 4)
                    pe.wait_ge(relu_ready, 4)
                else:
                    pe.wait_ge(logit_read, 2 * p)
                half = (slice(0, DH), slice(DH, 2 * DH))
                for i in range(2):
                    mm(bank[6 + i][:, 0:P], qT[half[i], p, 0:P], kT[half[i], p, 0:P], start=True, stop=True)
                for i in range(2):
                    mm(bank[6 + i][:, P:P + SEQ], qT[half[i], p, P:SEQ], kT[half[i], p, :], start=True, stop=True)\
                        .then_inc(logit_done, 1)

            def transpose_probs(h):
                pe.wait_ge(prob_ready, h + 1)
                if h == 0:
                    pe.wait_ge(mix_low, 4)
                else:
                    pe.wait_ge(pT_ready, h)
                for i in range(3):
                    ins = nc.tensor.transpose(bank[4][:, i * P:(i + 1) * P], prob[:, h % 2, i * P:(i + 1) * P], ident)
                ins.then_inc(pT_done, 1)

            def values(p):
                if p >= 1:
                    pe.wait_ge(att_low, p)
                for i in range(2):
                    pe.wait_ge(pT_ready, 2 * p + i + 1)
                    c = slice((2 * p + i) * DH, (2 * p + i + 1) * DH)
                    mm(bank[5][i * DH:(i + 1) * DH, 0:SEQ], vv[:, 0, c], pT[:, i, 0:SEQ], start=True, stop=False)
                for i in range(2):
                    c = slice((2 * p + i) * DH, (2 * p + i + 1) * DH)
                    mm(bank[5][i * DH:(i + 1) * DH, P:SEQ], vv[:, 1, c], pT[:, i, SEQ:SEQ + P], start=False, stop=True)\
                        .then_inc(pv_done, 1)

            pe.wait_ge(cst_loaded, 16)
            transposes(hs, (0, 1), lambda b, c: (h_ready, b + 1))
            pe.wait_ge(tp_low, 4)
            for n in range(N_PIECES):
                if n == P_Q + 1:
                    indexer_scores()
                if n in (20, 24, 28, 32):
                    logits((n - 20) // 4)
                if n == P_BA:
                    pe.wait_ge(att_low, 4)
                    pe.wait_ge(logit_read, NH)
                if n == P_WO:
                    transposes(hs, (0,), lambda b, c: (gated, 4 + 2 * (b + 1)))
                    pe.wait_ge(tp_low, 6)
                if n == P_WO + 1:
                    transposes(hs, (1,), lambda b, c: (gated, 8 + 2 * (b + 1)))
                if n == P_WO + 4:
                    pe.wait_ge(tp_low, 8)
                pe.wait_ge(low_ready, n + 1)
                if n < P_Q:
                    if n == 0:
                        pe.wait_ge(skew_ready, 4)
                    piece_idx(n)
                elif n < P_BP:
                    piece_group(n)
                elif n < P_BA:
                    piece_product(n, P_BP, 4, mixh, mixl, bank[0:4], branch_done, range(4))
                elif n < P_WO:
                    piece_product(n, P_BA, 4, atth, attl, bank[4:8], branch_done, ORDER)
                else:
                    piece_product(n, P_WO, 8, hTh, hTl, bank[4:8], wo_done, ORDER)
                if n == 21:
                    pooling()
                elif n == 23:
                    mixing()
                q, p = n % 4, n // 4
                if 24 <= n < 39:
                    if q in (0, 1):
                        transpose_probs(2 * (p - 6) + q)
                    elif q == 2:
                        values(p - 6)
            lo, hi = slice(0, SLOTS), slice(SLOTS, 2 * SLOTS)

            def bias1(bk, c):
                for part, c1 in ((lo, c), (hi, c + HALF)):
                    mm(bk[part, :], sel, b1s[:, c1:c1 + HALF], start=True, stop=False)

            def residual(q):
                mm(YSUM[q][:, :], ident, xs[:, q // 2, HALF * (q % 2):HALF * (q % 2 + 1)], start=True, stop=False,
                   skip_group_check=True)

            transposes(xs, (0, 1), lambda b, c: (x_ready, 2 * c + b + 1))
            residual(0)
            residual(2)
            pe.wait_ge(wr_ready, 1)
            for k in range(KD):
                if k % 4 == 0:
                    pe.wait_ge(tp_evac, 4)
                o = bank[2][(k % 4) * NE:(k % 4 + 1) * NE, 0:SEQ]
                ins = mm(o, wr[:, k, :], xT[:, k, :], start=k < 4, stop=k >= 4)
            ins.then_inc(parts_done, 1)
            pe.wait_ge(sel_ready, 1)
            pe.wait_ge(b1_loaded, 16)
            bias1(GA, 0)
            pe.wait_ge(parts_ready, 1)
            for b in range(TB):
                ins = mm(bank[3][:, b * NE:(b + 1) * NE], parts[:, b * P:(b + 1) * P], fold, start=True, stop=True)
            ins.then_inc(router_done, 1)
            bias1(UA, F)
            pe.wait_ge(routing, R_MASK)
            mm(bank[2][:, 0:NE], tri, emask[:, 0, :], start=True, stop=True)
            mm(bank[2][:, NE:2 * NE], ones, emask[:, 0, :], start=True, stop=False)
            mm(bank[2][:, NE:2 * NE], tri, emask[:, 1, :], start=False, stop=True)
            mm(bank[2][:, 2 * NE:3 * NE], ones, emask[:, 0, :], start=True, stop=False)
            mm(bank[2][:, 2 * NE:3 * NE], ones, emask[:, 1, :], start=False, stop=True).then_inc(rank_done, 1)
            residual(1)
            residual(3)
            pe.wait_ge(routing, R_COMB)
            for b in range(TB):
                ins = nc.tensor.transpose(bank[3][0:NE, b * P:(b + 1) * P], comb[:, b, 0:NE], ident)
            ins.then_inc(combT_done, 1)

            def gather():
                for k in range(KD):
                    for b in range(TB):
                        ins = mm(GATHER[:, k * SLOTS:(k + 1) * SLOTS], hs[:, b, k * P:(k + 1) * P], pick[:, b, :],
                                 start=b == 0, stop=b == TB - 1)
                ins.then_inc(gather_done, 1)

            def chunk_wait(u4, c):
                pe.wait_ge(chunk_loaded[c % ERING], u4 * (16 * TURNS) + 16 * (c // ERING + 1))

            def expert(r, g, i):
                e = g * GROUP + i
                u, u4 = r * NE + e, r * (NE // GROUP) + g
                first = isinstance(g, int)
                if not (first and i == 0):
                    pe.wait_ge(sel_ready, r * (NE + 1) + e + 1)
                    bias1(GA, 0)
                    bias1(UA, F)
                pe.wait_ge(xgT_ready, r * (NE + 1) + e + 1)
                for k in range(KD):
                    chunk_wait(u4, i * CHUNKS + k)
                    w = eslot[(i * CHUNKS + k) % ERING]
                    for bk, c in ((GA, 0), (UA, F)):
                        for part, c1 in ((lo, c), (hi, c + HALF)):
                            ins = mm(bk[part, :], xgT[:, k, :], w[:, c1:c1 + HALF], start=False, stop=k == KD - 1)
                    ins.then_inc(chunks_used, 1)
                if first:
                    if i == 0:
                        pe.wait_ge(combT_ready, 1)
                        pe.wait_ge(b2_loaded, 16)
                    mm(YSUM[i][:, :], combT[:, (i // 2) * P:(i // 2 + 1) * P], b2s[:, (i % 2) * HALF:(i % 2 + 1) * HALF],
                       start=False, stop=True, skip_group_check=True)
                pe.wait_ge(gpick_ready, u + 1)
                for b in range(TB):
                    ins = nc.tensor.transpose(YT[:, b * P:(b + 1) * P],
                                              gpick[:, b, :, :].rearrange("p u s -> p (u s)"), ident)
                ins.then_inc(gT_done, 1)
                pe.wait_ge(pick_ready, r * (NE + 1) + e + 2)
                gather()
                pe.wait_ge(act_ready, u + 1)
                for c in range(4):
                    ins = nc.tensor.transpose(GA[:, c * P:(c + 1) * P], act[:, c * P:(c + 1) * P], ident)
                ins.then_inc(actT_done, 1)
                pe.wait_ge(gT_ready, u + 1)
                pe.wait_ge(actT_ready, u + 1)
                for j in range(KD, CHUNKS):
                    chunk_wait(u4, i * CHUNKS + j)
                    w = eslot[(i * CHUNKS + j) % ERING].rearrange("p (k n) -> p k n", k=2)
                    for kk in range(2):
                        k = 2 * (j - KD) + kk
                        a_k = actT[:, (k % 4) * P + (k // 4) * SLOTS:(k % 4) * P + (k // 4 + 1) * SLOTS]
                        for part, c1 in ((lo, 0), (hi, HALF)):
                            ins = mm(YT[part, :], a_k, w[:, kk, c1:c1 + HALF], start=k == 0, stop=k == KD - 1)
                    ins.then_inc(chunks_used, 1)
                pe.wait_ge(y_ready, u + 1)
                for b in range(TB):
                    for c, part in enumerate((lo, hi)):
                        ins = mm(YSUM[2 * b + c][:, :], gT[part, b * P:(b + 1) * P], ys[part, :],
                                 start=False, stop=True, skip_group_check=True)
                    ins.then_inc(scattered, 1)

            def begin_round(r):
                pe.wait_ge(pick_ready, r * (NE + 1) + 1)
                gather()

            begin_round(0)
            for i in range(GROUP):
                expert(0, 0, i)
            with pe.Fori(1, NE // GROUP) as g:
                for i in range(GROUP):
                    expert(0, g, i)
            pe.wait_ge(count_ready, 1)
            most = pe.value_load(count[0:1, 0:1], min_val=0, max_val=SEQ)
            with pe.If(most > SLOTS):
                with pe.Fori(1, ROUNDS) as r:
                    pe.wait_ge(xgT_ready, r * (NE + 1))
                    begin_round(r)
                    with pe.Fori(0, NE // GROUP) as g:
                        for i in range(GROUP):
                            expert(r, g, i)


def constants():
    s = np.arange(P)[:, None]
    t = np.arange(P)[None, :]
    c = np.zeros((P, N_CONST), np.float32)
    c[:, K_ID:K_ID + P] = s == t
    c[:, K_TRI:K_TRI + P] = s < t
    c[:, K_ONE:K_ONE + P] = 1.0
    c[:, K_IOTA:K_IOTA + SLOTS] = np.arange(1, SLOTS + 1)
    c[:, K_FOLD:K_FOLD + NE] = s % NE == t[:, 0:NE]
    for g, w in enumerate(POOL_WINDOWS):
        near = (t - s >= 0) & (t - s < w)
        blocks = (near / np.minimum(t + 1, w) - (s == t),
                  (P + t - s < w) / w,
                  near / w - (s == t))
        for i, m in enumerate(blocks):
            at = K_BAND + (3 * g + i) * P
            c[:, at:at + P] = m
    return c


def bucket_rows():
    hot = np.zeros((BUCKETS, SEQ), np.float32)
    exact = BUCKETS // 2
    for c in range(SEQ):
        n = SEQ - 1 - c
        big = exact + int(np.float32(math.log(max(n, 1) / exact) / math.log(MAX_DIST / exact) * (BUCKETS - exact)))
        hot[n if n < exact else min(big, BUCKETS - 1), c] = 1.0
    return hot


def kernel(x, mix_norm, w_in, pool_w, pool_scale, w_branch_pool, w_branch_attn, rel_bias, w_out, ffn_norm,
           w_router, b_router, w1, b1, w2, b2, final_norm):
    import concourse.bacc as bacc
    from concourse.bass_utils import run_bass_kernel_spmd

    arrays = {
        "x": x[0], "mix_norm": mix_norm[0], "w_in": w_in[0], "pool_w": pool_w[0],
        "pool_scale": pool_scale[0].reshape(4, P).T, "w_branch_pool": w_branch_pool[0],
        "w_branch_attn": w_branch_attn[0], "rel_bias": rel_bias, "w_out": w_out[0],
        "ffn_norm": ffn_norm[0], "ffn_cols": ffn_norm[0].reshape(KD, P).T, "w_router": w_router[0], "b_router": b_router[0],
        "w1": w1[0], "b1": b1[0], "w2": w2[0], "b2": b2[0], "final_norm": final_norm,
        "consts": constants(), "bucket_hot": bucket_rows(),
    }
    arrays = {f"in_{n}": np.ascontiguousarray(a) for n, a in arrays.items()}
    nc = bacc.Bacc("TRN2", target_bir_lowering=False, num_devices=1)
    args = [nc.dram_tensor(n, a.shape, mybir.dt.from_np(a.dtype), kind="ExternalInput").ap() for n, a in arrays.items()]
    out = nc.dram_tensor("out", (SEQ, D), mybir.dt.float32, kind="ExternalOutput").ap()
    hybrid_block(nc, *args, out)
    r = run_bass_kernel_spmd(nc, [arrays], core_ids=[0])
    return r.results[0]["out"].reshape(1, SEQ, D)
```

```python
import concourse.bass as bass
from concourse import mybir
from contextlib import ExitStack
import math
import numpy as np

P = 128
SEQ, D = 256, 1024
TB = SEQ // P
KD = D // P
HALF = 512
POOL_WINDOWS = (2, 4, 8, 16)
NH, DH = 8, 64
NIH, DI = 4, 64
TOPK = SEQ // 4
BUCKETS, MAX_DIST = 32, 128
NE, TOPE = 32, 4
F = D
LIMIT, ALPHA, EPS = 7.0, 1.702, 1e-5
NEG_BIG = -1e30
MASKED, TAKEN = -3.0e38, -3.3e38
SLOTS = 64
ROUNDS = SEQ // SLOTS

C_POOL, C_Q, C_K, C_V = 0, 512, 1024, 1536
C_QI = 2048
C_GATE = C_QI + NIH * DI + DI + NIH
N_IDX = 3 * P

SLOT = 2048
FRING = 7
PIECE = SLOT // 2
LOOK = 4
ORDER = (0, 2, 1, 3)
N_PIECES = 52
P_IDX, P_Q, P_K, P_V, P_POOL, P_GATE, P_BP, P_BA, P_WO = 0, 4, 8, 12, 16, 20, 36, 40, 44
CHUNKS = 12
ERING = 16
PLACES = 21
GROUP = 4
PAIRS = NE // 2
TURNS = GROUP * CHUNKS // ERING

K_ID, K_TRI, K_ONE, K_IOTA, K_FOLD, K_BAND = 0, 128, 256, 384, 448, 488
N_CONST = K_BAND + 12 * 128
SKEW = 384
R_MASK, R_COMB, R_COUNT = 5, 9, 11


def hybrid_block(nc, x, mix_cols, w_in, pool_w, pool_scale, w_bp, w_ba, rel_bias, w_out,
                 ffn_norm, ffn_cols, w_router, b_router, w1, b1, w2, b2, final_norm, consts, bucket_hot, out):
    f32, f32r, i32 = mybir.dt.float32, mybir.dt.float32r, mybir.dt.int32
    ALU = mybir.AluOpType
    ACT = mybir.ActivationFunctionType
    X = mybir.AxisListType.X

    ctx = ExitStack()
    with ctx:
        def sem(name):
            return ctx.enter_context(nc.semaphore(name))

        base = -(-nc.sbuf_base // 64) * 64
        floats = (nc.sbuf_usable_end - base) // 4
        ctx.enter_context(nc.sbuf_tensor("arena", [P, (nc.sbuf_usable_end - nc.sbuf_base) // 4 - 32], f32))
        top = [0]

        def at(name, off, n, dt=f32, parts=P):
            assert off + n <= floats, (name, off + n, floats)
            return nc.alloc_sbuf_tensor_at(name, [parts, n], dt, offset=base + 4 * off)[:, :]

        def new(name, n, dt=f32):
            off = top[0]
            top[0] = off + -(-n // 8) * 8
            return at(name, off, n, dt)

        o_xs = top[0]
        xs = new("xs", TB * D).rearrange("p (b d) -> p b d", b=TB)
        hs = new("hs", TB * D).rearrange("p (b d) -> p b d", b=TB)
        cst = new("cst", K_BAND)
        ident, tri = cst[:, K_ID:K_ID + P], cst[:, K_TRI:K_TRI + P]
        ones, iota1 = cst[:, K_ONE:K_ONE + P], cst[:, K_IOTA:K_IOTA + SLOTS]
        fold = cst[:, K_FOLD:K_FOLD + NE + 1]
        o_masks = top[0]
        gfin = new("gfin", D)
        keepm = new("keepm", TB * SEQ).rearrange("p (b s) -> p b s", b=TB)
        poolw = new("poolw", 4 * P).rearrange("p (g d) -> p g d", g=4)
        gffn = new("gffn", D)
        ys = gffn.rearrange("p (c n) -> p c n", c=2)
        wr = new("wr", KD * NE).rearrange("p (k e) -> p k e", k=KD)
        br = new("br", NE)
        gcol = new("gcol", KD)
        mcol = new("mcol", KD)
        pscale = new("pscale", 4)
        wiT = new("wiT", SEQ)[DI:DI + NIH, :]
        wi = new("wi", TB * NIH).rearrange("p (b i) -> p b i", b=TB)
        stat = new("stat", 64)
        sq, var, std, rstd = stat[:, 0:4], stat[:, 4:6], stat[:, 6:8], stat[:, 8:10]
        lsum, linv, nlmax, warm = stat[:, 10:12], stat[:, 12:14], stat[:, 14:16], stat[:, 16:18]
        hmax, nhmax, hsum, hinv = (stat[:, 20 + 4 * i:24 + 4 * i].rearrange("p (r b) -> p r b", r=2) for i in range(4))
        m8 = stat[:, 40:48]

        o1 = top[0]
        r1 = new("r1", 7680)
        qT = r1[:, 0:1024].rearrange("p (b t) -> p b t", b=4)
        kT = r1[:, 1024:2048].rearrange("p (b t) -> p b t", b=4)
        qiT = r1[:, 2048:2560].rearrange("p (b t) -> p b t", b=2)
        kiT = r1[:, 2560:2816]
        relu = r1[:, 2816:3840].rearrange("p (r j s) -> p r j s", r=2, j=2)
        score = r1[:, 3840:4352].rearrange("p (b s) -> p b s", b=2)
        atth = at("atth", o1 + 2048, 1024, f32r).rearrange("p (g t) -> p g t", g=4)
        attl = at("attl", o1 + 3072, 1024, f32r).rearrange("p (g t) -> p g t", g=4)
        vv = r1[:, 4352:5376].rearrange("p (b c) -> p b c", b=2)
        logit = r1[:, 5376:6144].rearrange("p (r s) -> p r s", r=2)
        prob = r1[:, 6144:6912].rearrange("p (r s) -> p r s", r=2)
        pT = r1[:, 6912:7680].rearrange("p (r s) -> p r s", r=2)
        hot = r1[0:BUCKETS, 6144:6144 + SEQ]
        table = r1[0:BUCKETS, 6400:6400 + NH]
        b1s = r1[:, 2048:2560]
        b2s = r1[0:2 * NE, 2560:3072]
        xgT = [r1[:, o:o + 1024].rearrange("p (k s) -> p k s", k=KD) for o in (3072, 4352)]
        gT = r1[:, 4096:4352]
        gclip = r1[:, 5376:5888]
        act = r1[:, 5888:6400]
        actT = r1[:, 6400:6912]
        parts = r1[:, 6400:6656]
        combT = r1[0:2 * NE, 6912:7168]
        sel = r1[:, 7168:7232]
        iota_r = r1[:, 7232:7296]
        o3 = top[0]
        r3 = new("r3", 3584)
        uu = r3[:, 0:1024].rearrange("p (b c) -> p b c", b=2)
        pooledT = r3[:, 1024:2048].rearrange("p (g t) -> p g t", g=4)
        band = r3[:, 2048:3584].rearrange("p (m t) -> p m t", t=P)
        mixh = at("mixh", o3, 1024, f32r).rearrange("p (g t) -> p g t", g=4)
        mixl = at("mixl", o3 + 2048, 1024, f32r).rearrange("p (g t) -> p g t", g=4)
        rt = r3[:, 2048:]
        lg = rt[:, 0:80].rearrange("p (b e) -> p b e", b=2)
        lgt = rt[:, 80:160].rearrange("p (b e) -> p b e", b=2)
        top8 = rt[:, 160:176].rearrange("p (b e) -> p b e", b=2)
        rep8 = rt[:, 176:192].rearrange("p (b e) -> p b e", b=2)
        emask = rt[:, 192:256].rearrange("p (b e) -> p b e", b=2)
        eexp = rt[:, 256:320].rearrange("p (b e) -> p b e", b=2)
        comb = rt[:, 320:386].rearrange("p (b e) -> p b e", b=2)
        posn = rt[:, 386:454].rearrange("p (b e) -> p b e", b=2)
        cmax = rt[0:1, 454:455]
        uclip = rt[:, 464:976]
        pick = rt[:, 976:1232].rearrange("p (b s) -> p b s", b=TB)
        gpick = rt[:, 1232:1488].rearrange("p (b s) -> p b s", b=TB)
        count = at("count", o3 + 2048 + 456, 1, i32, 1)
        o_bias = top[0]
        bias = new("bias", NH * SEQ).rearrange("p (h s) -> p h s", h=NH)
        o_ring = top[0]
        ring = new("ring", FRING * SLOT).rearrange("p (r n) -> p r n", r=FRING)
        o_gates = top[0]
        gates = new("gates", TB * 2 * D).rearrange("p (i b c) -> p i b c", i=2, b=TB)
        skew = at("skew", o_gates, SKEW)[0:NH, :]
        o_split = top[0]
        wh = new("wh", LOOK * PIECE, f32r).rearrange("p (i n) -> p i n", i=LOOK)
        wl = new("wl", LOOK * PIECE, f32r).rearrange("p (i n) -> p i n", i=LOOK)
        o_hT = top[0]
        hTh = new("hTh", KD * SEQ, f32r).rearrange("p (k t) -> p k t", k=KD)
        hTl = new("hTl", KD * SEQ, f32r).rearrange("p (k t) -> p k t", k=KD)
        xT = at("xT", o_hT, KD * SEQ).rearrange("p (k t) -> p k t", k=KD)

        def ring_at(pieces):
            return o_ring + SLOT * ((pieces // 2 - 1) % FRING)

        bank = [ctx.enter_context(nc.psum_tensor(f"bank{i}", [P, HALF], f32)) for i in range(8)]
        GA, UA, GATHER, YT = bank[0:4]
        YSUM = bank[4:8]

        skew_dram = nc.dram_tensor("skew_dram", (P, NH * SKEW), f32, kind="Internal").ap()

        ring_loaded = [sem(f"ring_loaded{i}") for i in range(FRING)]
        chunk_loaded = [sem(f"chunk_loaded{i}") for i in range(PLACES)]
        chunks_used = sem("chunks_used")
        high_ready, low_ready, piece_used = sem("high_ready"), sem("low_ready"), sem("piece_used")
        x_loaded = [sem(f"x_loaded{b}") for b in range(TB)]
        cst_loaded = sem("cst_loaded")
        mcol_loaded, gffn_loaded, gfin_loaded = sem("mcol_loaded"), sem("gffn_loaded"), sem("gfin_loaded")
        table_loaded, band_loaded, poolw_loaded = sem("table_loaded"), sem("band_loaded"), sem("poolw_loaded")
        router_loaded, b1_loaded, b2_loaded = sem("router_loaded"), sem("b1_loaded"), sem("b2_loaded")
        warm_ready = sem("warm_ready")
        skew_done, skew_ready = sem("skew_done"), sem("skew_ready")
        skew_saved, bias_loaded = sem("skew_saved"), sem("bias_loaded")
        squares_ready, var_ready, std_ready = sem("squares_ready"), sem("var_ready"), sem("std_ready")
        rstd_ready, h_ready = sem("rstd_ready"), sem("h_ready")
        tp_done, tp_high, tp_low, tp_evac = sem("tp_done"), sem("tp_high"), sem("tp_low"), sem("tp_evac")
        idx_ready = sem("idx_ready")
        sc_done, relu_ready, score_ready = sem("sc_done"), sem("relu_ready"), sem("score_ready")
        causal_ready, taken_ready, kept_ready = sem("causal_ready"), sem("taken_ready"), sem("kept_ready")
        keepm_ready = sem("keepm_ready")
        half_evac, gate_ready = sem("half_evac"), sem("gate_ready")
        pool_done, pool_evac, mix_high, mix_low = sem("pool_done"), sem("pool_evac"), sem("mix_high"), sem("mix_low")
        logit_done, logit_read = sem("logit_done"), sem("logit_read")
        hmax_ready, nhmax_ready, exp_ready = sem("hmax_ready"), sem("nhmax_ready"), sem("exp_ready")
        hinv_ready, prob_ready = sem("hinv_ready"), sem("prob_ready")
        pT_done, pT_ready, pv_done = sem("pT_done"), sem("pT_ready"), sem("pv_done")
        att_high, att_low = sem("att_high"), sem("att_low")
        branch_done, gated, merged = sem("branch_done"), sem("gated"), sem("merged")
        wo_done, x_ready = sem("wo_done"), sem("x_ready")
        wr_ready, parts_done, parts_ready = sem("wr_ready"), sem("parts_done"), sem("parts_ready")
        router_done, routing, nlmax_ready = sem("router_done"), sem("routing"), sem("nlmax_ready")
        eexp_ready, rank_done = sem("eexp_ready"), sem("rank_done")
        counts_done = sem("counts_done")
        combT_done, combT_ready = sem("combT_done"), sem("combT_ready")
        count_ready = sem("count_ready")
        sel_ready = sem("sel_ready")
        pick_ready, gather_done, xgT_ready = sem("pick_ready"), sem("gather_done"), sem("xgT_ready")
        gpick_ready, gT_done, gT_ready = sem("gpick_ready"), sem("gT_done"), sem("gT_ready")
        gclip_ready, sig_ready, act_ready = sem("gclip_ready"), sem("sig_ready"), sem("act_ready")
        uclip_ready, gu_ready = sem("uclip_ready"), sem("gu_ready")
        actT_done, actT_ready = sem("actT_done"), sem("actT_ready")
        y_ready, y1_ready, scattered = sem("y_ready"), sem("y1_ready"), sem("scattered")
        iota_ready = sem("iota_ready")
        out_saved = sem("out_saved")

        END = GROUP * CHUNKS
        first = [
            (o_bias, END),
            (o1, END - ERING),
            (o_masks, END - ERING),
            (ring_at(40), END),
            (ring_at(42), END),
            (o1 + 4352, 0),
            (o3, END - ERING),
            (ring_at(44), END),
            (o_gates, END),
            (ring_at(46), END),
            (o_gates + SLOT, END),
            (ring_at(48), END),
            (ring_at(50), END),
            (ring_at(52), END),
            (o_split, END),
            (o_split + 2 * SLOT, END),
            (o_split + SLOT, END),
            (o_split + 3 * SLOT, END),
            (o_hT + SLOT, END),
            (o_hT, END),
            (o_xs, END - ERING),
        ]
        assert len(first) == PLACES
        place = [at(f"place{i}", off, SLOT) for i, (off, _) in enumerate(first)]
        plan = [(i, 1, None) for i in range(PLACES)]
        free = list(range(PLACES))
        for c in range(PLACES, END):
            while first[plan[free[0]][0]][1] <= c:
                free.pop(0)
            former = free.pop(0)
            plan.append((plan[former][0], plan[former][1] + 1, former))
            free.append(c)
        slots = plan[END - ERING:]
        assert len({p[0] for p in slots}) == ERING
        gain_free = 1 + max(c for c, p in enumerate(plan) if first[p[0]][0] == o_masks)

        block = ctx.enter_context(nc.Block())

        w_in_k = w_in.rearrange("(k p) n -> p k n", p=P)
        w1_k = w1.rearrange("e (k p) n -> e p k n", p=P)
        w2_k = w2.rearrange("e (k p) n -> e p k n", p=P)

        def piece_cols(t, n):
            v = t.rearrange("p (k n) -> p k n", k=2)
            return v[:, :, 0:N_IDX] if n < P_Q else v

        def ring_piece(n):
            return piece_cols(ring[:, (n // 2) % FRING, (n % 2) * PIECE:(n % 2 + 1) * PIECE], n)

        @block.sync
        def _(sp):
            for b in range(TB):
                sp.dma_start(xs[:, b, :], x[b * P:(b + 1) * P, :]).then_inc(x_loaded[b], 16)

            def load(use, src, k, n):
                if use >= FRING:
                    sp.wait_ge(low_ready, 2 * (use - FRING) + 2)
                dst = ring[:, use % FRING, :].rearrange("p (k n) -> p k n", k=k)[:, :, 0:n]
                sp.dma_start(dst, src).then_inc(ring_loaded[use % FRING], 16)

            use = 0
            for c0, n in ((C_QI, N_IDX), (C_Q, 512), (C_K, 512), (C_V, 512), (C_POOL, 512),
                          *((C_GATE + 512 * i, 512) for i in range(4))):
                for i in range(2):
                    load(use, w_in_k[:, 4 * i:4 * i + 4, c0:c0 + n], 4, n)
                    use += 1
                    if use == 1:
                        sp.dma_start(hot, bucket_hot).then_inc(table_loaded, 16)
                        sp.dma_start(table, rel_bias).then_inc(table_loaded, 16)
            for w in (w_bp, w_ba, w_out):
                wk = w.rearrange("(k p) n -> p k n", p=P)
                for i in range(wk.shape[1] // 2):
                    load(use, wk[:, 2 * i:2 * i + 2, :], 2, D)
                    use += 1

            def chunk(e, j, slot, loaded):
                if j < KD:
                    dst, src = slot, w1_k[e, :, j, :]
                else:
                    dst = slot.rearrange("p (k n) -> p k n", k=2)
                    src = w2_k[e, :, 2 * (j - KD):2 * (j - KD) + 2, :]
                sp.dma_start(dst, src).then_inc(loaded, 16)

            former_use = (
                (logit_read, NH),
                (logit_done, NH),
                (hmax_ready, 2 * NH),
                (low_ready, 40),
                (low_ready, 42),
                (att_low, NH // 2),
                (piece_used, P_BA),
                (low_ready, 44),
                (gated, 4),
                (low_ready, 46),
                (merged, 4),
                (low_ready, 48),
                (low_ready, 50),
                (low_ready, 52),
                (piece_used, N_PIECES - 2),
                (piece_used, N_PIECES - 2),
                (piece_used, N_PIECES),
                (piece_used, N_PIECES),
                (piece_used, N_PIECES),
                (parts_done, 1),
                (gather_done, 1),
            )
            for c in range(END):
                if c < PLACES:
                    sp.wait_ge(*former_use[c])
                else:
                    sp.wait_ge(chunks_used, plan[c][2] + 1)
                chunk(c // CHUNKS, c % CHUNKS, place[plan[c][0]], chunk_loaded[plan[c][0]])

            def load_group(r, g):
                for c in range(GROUP * CHUNKS):
                    i = slots[c % ERING][0]
                    sp.wait_ge(chunks_used, (r * NE + g * GROUP) * CHUNKS + c - ERING + 1)
                    chunk(g * GROUP + c // CHUNKS, c % CHUNKS, place[i], chunk_loaded[i])

            with sp.Fori(1, NE // GROUP) as g:
                load_group(0, g)
            sp.wait_ge(count_ready, 1)
            most = sp.value_load(count[0:1, 0:1], min_val=0, max_val=SEQ)
            with sp.If(most > SLOTS):
                with sp.Fori(1, ROUNDS) as r:
                    with sp.Fori(0, NE // GROUP) as g:
                        load_group(r, g)
            for q in range(4):
                b, half = q // 2, slice(q % 2 * HALF, (q % 2 + 1) * HALF)
                sp.wait_ge(h_ready, 2 * TB + q + 1)
                sp.dma_start(out[b * P:(b + 1) * P, half], hs[:, b, half]).then_inc(out_saved, 16)
            sp.wait_ge(out_saved, 16 * 4)

        @block.gpsimd
        def _(pool):
            nc.gpsimd.memset(warm, 1.0).then_inc(warm_ready, 1)
            nc.gpsimd.memset(skew[:, SEQ:SKEW], 0.0).then_inc(warm_ready, 1)

            def causal(ready, t, b, fill, done):
                n = P * (b + 1)
                pool.wait_ge(ready, b + 1)
                nc.gpsimd.affine_select(out=t[:, b, 0:n], in_=t[:, b, 0:n], compare_op=ALU.is_ge, fill=fill,
                                        base=P * b, pattern=[[-1, n]], channel_multiplier=1).then_inc(done, 1)

            for b in range(TB):
                causal(score_ready, score, b, MASKED, causal_ready)
            causal(kept_ready, keepm, 0, NEG_BIG, keepm_ready)
            pool.wait_ge(piece_used, P_POOL - 4)
            pool.wait_ge(skew_ready, 1)
            pool.wait_ge(warm_ready, 2)
            pool.dma_start(skew_dram.rearrange("p (h s) -> h p s", h=NH),
                           skew.unsqueeze(1).to_broadcast([NH, P, SKEW])).then_inc(skew_saved, 16)
            pool.wait_ge(skew_saved, 16)
            skewed = bass.AP(tensor=skew_dram.tensor, offset=P - 1, ap=[[NH * SKEW - 1, P], [SKEW, NH], [1, SEQ]])
            pool.dma_start(bias, skewed).then_inc(bias_loaded, 16)
            pool.dma_start(band, consts[:, K_BAND:].rearrange("p (m t) -> p m t", t=P)).then_inc(band_loaded, 16)
            pool.dma_start(poolw, pool_w.rearrange("g c d -> c g d")).then_inc(poolw_loaded, 16)
            pool.dma_start(pscale, pool_scale).then_inc(poolw_loaded, 16)
            pool.dma_start(gffn, ffn_norm.partition_broadcast(P)).then_inc(gffn_loaded, 16)
            pool.dma_start(wr, w_router.rearrange("(k p) e -> p k e", p=P)).then_inc(router_loaded, 16)
            pool.dma_start(br, b_router.partition_broadcast(P)).then_inc(router_loaded, 16)
            pool.dma_start(gcol, ffn_cols).then_inc(router_loaded, 16)
            causal(kept_ready, keepm, 1, NEG_BIG, keepm_ready)
            for n, q in enumerate(ORDER):
                half = slice(HALF * (q % 2), HALF * (q % 2 + 1))
                m = hs[:, q // 2, half]
                pool.wait_ge(gated, 4 + n + 1)
                nc.gpsimd.tensor_tensor(m, m, gates[:, 1, q // 2, half], ALU.add).then_inc(merged, 1)
            pool.wait_ge(piece_used, P_WO)
            pool.dma_start(b1s, b1).then_inc(b1_loaded, 16)
            pool.dma_start(b2s, b2).then_inc(b2_loaded, 16)
            pool.wait_ge(chunks_used, gain_free)
            pool.dma_start(gfin, final_norm.partition_broadcast(P)).then_inc(gfin_loaded, 16)

        @block.scalar
        def _(a):
            a.dma_start(cst, consts[:, 0:K_BAND]).then_inc(cst_loaded, 16)
            a.dma_start(mcol, mix_cols).then_inc(mcol_loaded, 16)

            def squares(i, order):
                for n, q in enumerate(order):
                    b, c = q // 2, q % 2
                    half = slice(c * HALF, (c + 1) * HALF)
                    if i == 0:
                        a.wait_ge(x_loaded[b], 16)
                    elif i == 1:
                        a.wait_ge(x_ready, n + 1)
                    else:
                        a.wait_ge(scattered, 4 * PAIRS - 3 + n)
                    nc.scalar.activation(hs[:, b, half], YSUM[q][:, :] if i == 2 else xs[:, b, half], ACT.Square,
                                         accum_out=sq[:, q:q + 1]).then_inc(squares_ready, 1)
                    if i != 1 and n % 2:
                        root(i, b)

            def root(i, b):
                a.wait_ge(var_ready, 2 * i + b + 1)
                nc.scalar.activation(std[:, b:b + 1], var[:, b:b + 1], ACT.Sqrt, scale=1.0 / D).then_inc(std_ready, 1)

            def fetch_root_table():
                nc.scalar.activation(warm[:, 0:1], warm[:, 1:2], ACT.Sqrt)

            def high(n):
                use = n // 2
                a.wait_ge(ring_loaded[use % FRING], 16 * (use // FRING + 1))
                if n >= LOOK:
                    a.wait_ge(piece_used, n - LOOK + 1)
                nc.scalar.activation(piece_cols(wh[:, n % LOOK, :], n), ring_piece(n), ACT.Copy).then_inc(high_ready, 1)

            def normed_high():
                a.wait_ge(mcol_loaded, 16)
                for k in range(KD):
                    if k % 2 == 0:
                        a.wait_ge(tp_done, k // 2 + 1)
                    ins = nc.scalar.activation(hTh[:, k, :], bank[k // 2][:, (k % 2) * SEQ:(k % 2 + 1) * SEQ], ACT.Copy,
                                               scale=mcol[:, k:k + 1])
                    if k % 2:
                        ins.then_inc(tp_high, 1)

            def merged_high(banks):
                for j in banks:
                    a.wait_ge(tp_done, 4 + j + 1)
                    nc.scalar.activation(hTh[:, 2 * j:2 * j + 2, :],
                                         bank[j][:, :].rearrange("p (k t) -> p k t", k=2), ACT.Copy)\
                        .then_inc(tp_high, 1)

            def indexer_operands():
                a.wait_ge(piece_used, P_Q)
                for half in (slice(0, DI), slice(DI, 2 * DI)):
                    nc.scalar.activation(kiT[half, :], bank[5][0:DI, 0:SEQ], ACT.Copy).then_inc(idx_ready, 1)
                nc.scalar.activation(wiT, bank[5][DI:DI + NIH, 0:SEQ], ACT.Copy).then_inc(idx_ready, 1)
                nc.scalar.activation(qiT, bank[4][:, :].rearrange("p (b t) -> p b t", b=2), ACT.Copy)\
                    .then_inc(idx_ready, 1)

            def indexer_relu():
                for b in range(TB):
                    n = P * (b + 1)
                    a.wait_ge(sc_done, b + 1)
                    if b == 0:
                        nc.scalar.activation(wi, bank[5][:, 3 * P:3 * P + TB * NIH].rearrange("p (b i) -> p b i", b=TB),
                                             ACT.Copy).then_inc(idx_ready, 1)
                    else:
                        a.wait_ge(score_ready, 1)
                    for r in range(2):
                        src = bank[4 + 2 * b + r][:, :].rearrange("p (j s) -> p j s", j=2)[:, :, 0:n]
                        nc.scalar.activation(relu[:, r, :, 0:n], src, ACT.Relu,
                                             scale=float(DI ** -0.5 * NIH ** -0.5)).then_inc(relu_ready, 1)

            def group_out(g):
                a.wait_ge(piece_used, P_Q + 4 * (g + 1))
                for b in range(2):
                    src = bank[2 * (g % 2) + b][:, :]
                    pair = src.rearrange("p (b t) -> p b t", b=2)
                    if g < 2:
                        nc.scalar.activation((qT if g == 0 else kT)[:, 2 * b:2 * b + 2, :], pair, ACT.Copy)\
                            .then_inc(half_evac, 1)
                    elif g < 4:
                        nc.scalar.activation((vv if g == 2 else uu)[:, b, :], src, ACT.Copy).then_inc(half_evac, 1)
                    else:
                        if g == 4:
                            a.wait_ge(skew_saved, 16)
                        nc.scalar.activation(gates[:, (g - 4) // 2, b, HALF * (g % 2):HALF * (g % 2 + 1)], src, ACT.Copy)\
                            .then_inc(half_evac, 1)

            def pooled():
                for i in range(2):
                    a.wait_ge(pool_done, i + 1)
                    nc.scalar.activation(pooledT[:, 2 * i:2 * i + 2, :],
                                         bank[4 + i][:, :].rearrange("p (g t) -> p g t", g=2), ACT.Copy)\
                        .then_inc(pool_evac, 1)

            def mixed_high():
                a.wait_ge(poolw_loaded, 32)
                for g in range(4):
                    a.wait_ge(pool_done, 2 + g // 2 + 1)
                    nc.scalar.activation(mixh[:, g, :], bank[4 + g // 2][:, (g % 2) * SEQ:(g % 2 + 1) * SEQ], ACT.Copy,
                                         scale=pscale[:, g:g + 1]).then_inc(mix_high, 1)

            def exps(h):
                r = h % 2
                a.wait_ge(nhmax_ready, h + 1)
                if h >= 2:
                    a.wait_ge(pT_done, h - 1)
                for b, (s0, n) in enumerate(((0, P), (P, SEQ))):
                    nc.scalar.activation(prob[:, r, s0:s0 + n], logit[:, r, s0:s0 + n], ACT.Exp,
                                         bias=nhmax[:, r, b:b + 1], accum_out=hsum[:, r, b:b + 1])\
                        .then_inc(exp_ready, 1)

            def probs_transposed(h):
                a.wait_ge(pT_done, h + 1)
                if h >= 2:
                    a.wait_ge(pv_done, h - 1)
                nc.scalar.activation(pT[:, h % 2, :], bank[4][:, 0:384], ACT.Copy).then_inc(pT_ready, 1)

            def attended_high(pr):
                a.wait_ge(pv_done, 2 * pr + 2)
                nc.scalar.activation(atth[:, pr, :], bank[5][:, 0:SEQ], ACT.Copy).then_inc(att_high, 1)

            a.wait_ge(warm_ready, 1)
            fetch_root_table()
            squares(0, range(4))
            for n in range(N_PIECES):
                high(n)
                if n == 1:
                    normed_high()
                elif n == P_Q + 3:
                    indexer_operands()
                elif n == P_Q + 4:
                    indexer_relu()
                elif n in (11, 15, 19, 23, 31, 35):
                    group_out((n - 11) // 4)
                elif n == 25:
                    pooled()
                elif n == 27:
                    mixed_high()
                    group_out(4)
                elif n == 39:
                    group_out(7)
                elif n in (45, 49):
                    merged_high((0, 1) if n == 45 else (2, 3))
                q, p = n % 4, n // 4
                if 24 <= n < 40 and q in (0, 1):
                    exps(2 * (p - 6) + q)
                if 28 <= n < 44:
                    if q in (0, 1):
                        probs_transposed(2 * (p - 7) + q)
                    elif q == 2:
                        attended_high(p - 7)
                if n in (39, 41):
                    a.wait_ge(half_evac, 16)
                    for b in range(TB):
                        nc.scalar.activation(gates[:, (n - 39) // 2, b, :], gates[:, (n - 39) // 2, b, :], ACT.Sigmoid)\
                            .then_inc(gate_ready, 1)
            fetch_root_table()
            squares(1, ORDER)
            for j in (2, 3):
                a.wait_ge(tp_done, 8 + j + 1)
                nc.scalar.activation(xT[:, 2 * j:2 * j + 2, :],
                                     bank[j][:, :].rearrange("p (k t) -> p k t", k=2), ACT.Copy).then_inc(tp_evac, 1)
            for b in range(TB):
                root(1, b)
            a.wait_ge(parts_done, 1)
            nc.scalar.activation(parts, bank[2][:, 0:SEQ], ACT.Copy).then_inc(parts_ready, 1)
            a.wait_ge(nlmax_ready, 1)
            for b in range(TB):
                nc.scalar.activation(eexp[:, b, :], lg[:, b, 0:NE], ACT.Exp, bias=nlmax[:, b:b + 1])\
                    .then_inc(eexp_ready, 1)
            def copy_xgT(halves, h, buffer):
                a.wait_ge(gather_done, halves)
                nc.scalar.activation(xgT[buffer][:, 4 * h:4 * h + 4, :],
                                     GATHER[:, :].rearrange("p (k s) -> p k s", k=4), ACT.Copy).then_inc(xgT_ready, 1)

            def experts_round(r):
                copy_xgT(r * (2 * PAIRS + 2) + 1, 0, 0)
                if isinstance(r, int):
                    a.wait_ge(combT_done, 1)
                    for half in (slice(0, NE), slice(NE, 2 * NE)):
                        nc.scalar.activation(combT[half, :], bank[3][0:NE, 0:SEQ], ACT.Copy).then_inc(combT_ready, 1)
                copy_xgT(r * (2 * PAIRS + 2) + 2, 1, 0)
                with a.Fori(0, NE // GROUP) as g:
                    for i in range(GROUP):
                        u = r * NE + g * GROUP + i
                        a.wait_ge(gclip_ready, u + 1)
                        nc.scalar.activation(act, gclip, ACT.Sigmoid, scale=ALPHA).then_inc(sig_ready, 1)
                        if i % 2 == 0:
                            a.wait_ge(gT_done, r * PAIRS + g * (GROUP // 2) + i // 2 + 1)
                            nc.scalar.activation(gT, YT[:, 0:SEQ], ACT.Copy).then_inc(gT_ready, 1)
                        copy_xgT(r * (2 * PAIRS + 2) + g * GROUP + i + 3, i % 2, (i // 2 + 1) % 2)
                        a.wait_ge(actT_done, u + 1)
                        nc.scalar.activation(actT, GA[:, :], ACT.Copy).then_inc(actT_ready, 1)
                        a.wait_ge(chunks_used, u * CHUNKS + CHUNKS)
                        own = slice((i % 2) * SLOTS, (i % 2 + 1) * SLOTS)
                        nc.scalar.activation(ys[own, 0, :], YT[0:SLOTS, :], ACT.Copy).then_inc(y_ready, 1)

            experts_round(0)
            a.wait_ge(count_ready, 1)
            most = a.value_load(count[0:1, 0:1], min_val=0, max_val=SEQ)
            with a.If(most > SLOTS):
                with a.Fori(1, ROUNDS) as r:
                    experts_round(r)
                a.wait_ge(scattered, ROUNDS * 4 * PAIRS)
            fetch_root_table()
            squares(2, range(4))

        @block.vector
        def _(v):
            def square_sum(i, b, squares_needed):
                v.wait_ge(squares_ready, 4 * i + squares_needed)
                nc.vector.tensor_scalar(var[:, b:b + 1], sq[:, 2 * b:2 * b + 1], sq[:, 2 * b + 1:2 * b + 2], D * EPS,
                                        ALU.add, ALU.add).then_inc(var_ready, 1)

            def inverse(i, b):
                v.wait_ge(std_ready, 2 * i + b + 1)
                nc.vector.reciprocal(rstd[:, b:b + 1], std[:, b:b + 1]).then_inc(rstd_ready, 1)
                v.wait_ge(rstd_ready, 2 * i + b + 1)

            def result(b, c):
                half = slice(c * HALF, (c + 1) * HALF)
                nc.vector.scalar_tensor_tensor(out=hs[:, b, half], in0=YSUM[2 * b + c][:, :], scalar=rstd[:, b:b + 1],
                                               in1=gfin[:, half], op0=ALU.mult, op1=ALU.mult).then_inc(h_ready, 1)

            def low(n):
                v.wait_ge(high_ready, n + 1)
                nc.vector.tensor_tensor(piece_cols(wl[:, n % LOOK, :], n), ring_piece(n),
                                        piece_cols(wh[:, n % LOOK, :], n).bitcast(f32), ALU.subtract)\
                    .then_inc(low_ready, 1)

            def normed_low():
                v.wait_ge(mcol_loaded, 16)
                for k in range(KD):
                    if k % 2 == 0:
                        v.wait_ge(tp_high, k // 2 + 1)
                    ins = nc.vector.scalar_tensor_tensor(out=hTl[:, k, :], in0=bank[k // 2][:, (k % 2) * SEQ:(k % 2 + 1) * SEQ],
                                                         scalar=mcol[:, k:k + 1], in1=hTh[:, k, :].bitcast(f32),
                                                         op0=ALU.mult, op1=ALU.subtract)
                    if k % 2:
                        ins.then_inc(tp_low, 1)

            def merged_low(banks):
                for j in banks:
                    v.wait_ge(tp_high, 4 + j + 1)
                    k = slice(2 * j, 2 * j + 2)
                    nc.vector.tensor_tensor(hTl[:, k, :], bank[j][:, :].rearrange("p (k t) -> p k t", k=2),
                                            hTh[:, k, :].bitcast(f32), ALU.subtract).then_inc(tp_low, 1)

            steps = [0]

            def taking(ins):
                ins.then_inc(taken_ready, 1)
                steps[0] += 1
                v.wait_ge(taken_ready, steps[0])

            def scores():
                for b in range(TB):
                    n = P * (b + 1)
                    v.wait_ge(idx_ready, 5)
                    v.wait_ge(relu_ready, 2 * b + 2)
                    for i in range(NIH):
                        rl, w = relu[:, i % 2, i // 2, 0:n], wi[:, b, i:i + 1]
                        if i == 0:
                            ins = nc.vector.tensor_scalar(score[:, b, 0:n], rl, w, None, ALU.mult)
                        else:
                            ins = nc.vector.scalar_tensor_tensor(out=score[:, b, 0:n], in0=rl, scalar=w,
                                                                 in1=score[:, b, 0:n], op0=ALU.mult, op1=ALU.add)
                        if i < NIH - 1:
                            taking(ins)
                    ins.then_inc(score_ready, 1)

            def take_quarter(b, last):
                n = P * (b + 1)
                v.wait_ge(causal_ready, b + 1)
                for _ in range(TOPK // 4 // 8):
                    taking(nc.vector.max(m8, score[:, b, 0:n]))
                    taking(nc.vector.match_replace(score[:, b, 0:n], m8, score[:, b, 0:n], TAKEN))
                if last:
                    nc.vector.tensor_scalar(keepm[:, b, 0:n], score[:, b, 0:n], (MASKED + TAKEN) / 2, NEG_BIG,
                                            ALU.is_ge, ALU.mult).then_inc(kept_ready, 1)

            def mixed_low():
                for g in range(4):
                    v.wait_ge(mix_high, g // 2 * 2 + 2)
                    nc.vector.scalar_tensor_tensor(out=mixl[:, g, :], in0=bank[4 + g // 2][:, (g % 2) * SEQ:(g % 2 + 1) * SEQ],
                                                   scalar=pscale[:, g:g + 1], in1=mixh[:, g, :].bitcast(f32),
                                                   op0=ALU.mult, op1=ALU.subtract).then_inc(mix_low, 1)

            def softmax_in(h):
                r = h % 2
                lb = bank[6 + r]
                v.wait_ge(logit_done, h + 1)
                if h == 0:
                    v.wait_ge(bias_loaded, 16)
                    v.wait_ge(keepm_ready, 2)
                if h >= 2:
                    v.wait_ge(exp_ready, 2 * (h - 1))
                for s0, n, c0 in ((0, P, P), (P, SEQ, 0)):
                    ins = nc.vector.scalar_tensor_tensor(out=logit[:, r, s0:s0 + n], in0=lb[:, s0:s0 + n],
                                                         scalar=float(DH ** -0.5), in1=bias[:, h, c0:c0 + n],
                                                         op0=ALU.mult, op1=ALU.add)
                ins.then_inc(logit_read, 1)
                v.wait_ge(logit_read, h + 1)
                for b, (s0, n) in enumerate(((0, P), (P, SEQ))):
                    nc.vector.tensor_tensor_reduce(out=logit[:, r, s0:s0 + n], in0=logit[:, r, s0:s0 + n],
                                                   in1=keepm[:, b, 0:n], scale=1.0, scalar=-3.4e38,
                                                   op0=ALU.add, op1=ALU.max, accum_out=hmax[:, r, b:b + 1])\
                        .then_inc(hmax_ready, 1)
                v.wait_ge(hmax_ready, 2 * h + 2)
                nc.vector.tensor_scalar(nhmax[:, r, :], hmax[:, r, :], -1.0, None, ALU.mult).then_inc(nhmax_ready, 1)

            def softmax_out(h):
                r = h % 2
                v.wait_ge(exp_ready, 2 * h + 2)
                nc.vector.reciprocal(hinv[:, r, :], hsum[:, r, :]).then_inc(hinv_ready, 1)
                v.wait_ge(hinv_ready, h + 1)
                for b, (s0, n) in enumerate(((0, P), (P, SEQ))):
                    ins = nc.vector.tensor_scalar(prob[:, r, s0:s0 + n], prob[:, r, s0:s0 + n],
                                                  hinv[:, r, b:b + 1], None, ALU.mult)
                ins.then_inc(prob_ready, 1)

            def attended_low(pr):
                v.wait_ge(att_high, pr + 1)
                nc.vector.tensor_tensor(attl[:, pr, :], bank[5][:, 0:SEQ], atth[:, pr, :].bitcast(f32), ALU.subtract)\
                    .then_inc(att_low, 1)

            def gate_quarter(i, n):
                q = ORDER[n] if i else n
                b, half = q // 2, slice(HALF * (q % 2), HALF * (q % 2 + 1))
                if n < 3:
                    v.wait_ge(branch_done, 3 * i + n + 1)
                else:
                    v.wait_ge(piece_used, (P_BA, P_WO)[i])
                v.wait_ge(gate_ready, 2 * i + b + 1)
                g = gates[:, i, b, half]
                nc.vector.tensor_tensor(g if i else hs[:, b, half], bank[4 * i + q][:, :], g, ALU.mult)\
                    .then_inc(gated, 1)

            for b in range(TB):
                v.wait_ge(x_loaded[b], 16)
                square_sum(0, b, 2 * b + 2)
                inverse(0, b)
                nc.vector.tensor_scalar(hs[:, b, :], xs[:, b, :], rstd[:, b:b + 1], None, ALU.mult).then_inc(h_ready, 1)
            for n in range(N_PIECES):
                low(n)
                if n == 1:
                    normed_low()
                elif n == 3:
                    v.wait_ge(skew_done, 1)
                    nc.vector.tensor_copy(skew[:, 0:SEQ], bank[6][0:NH, 0:SEQ]).then_inc(skew_ready, 1)
                elif n == P_Q + 4:
                    scores()
                elif P_K < n <= P_K + 8:
                    take_quarter((n - P_K - 1) // 4, n % 4 == 0)
                elif n == 27:
                    mixed_low()
                elif n == 49:
                    merged_low((2, 3))
                q, p = n % 4, n // 4
                if 23 <= n < 37:
                    if q == 3:
                        softmax_in(2 * (p - 5))
                    elif q == 0:
                        softmax_in(2 * (p - 6) + 1)
                if 25 <= n < 39 and q in (1, 2):
                    softmax_out(2 * (p - 6) + q - 1)
                if 30 <= n < 43 and q == 2:
                    attended_low(p - 7)
                if n == 43:
                    for i in range(4):
                        gate_quarter(0, i)
                    for i in range(2):
                        gate_quarter(1, i)
                elif n == 45:
                    merged_low((0, 1))
                    for i in (2, 3):
                        gate_quarter(1, i)
            nc.vector.memset(lg[:, :, NE:], MASKED)
            nc.vector.memset(posn, 0.0)
            nc.vector.memset(comb, 0.0)
            nc.vector.memset(rep8, MASKED)
            nc.vector.tensor_copy(iota_r, iota1).then_inc(iota_ready, 1)

            def make_sel(e):
                nc.vector.tensor_copy(sel, fold[:, bass.ds(e, 1)].to_broadcast([P, SLOTS])).then_inc(sel_ready, 1)

            v.wait_ge(router_loaded, 48)
            nc.vector.tensor_tensor(wr, wr, gcol.unsqueeze(2).to_broadcast([P, KD, NE]), ALU.mult).then_inc(wr_ready, 1)
            make_sel(0)
            for n, q in enumerate(ORDER):
                if n < 3:
                    v.wait_ge(wo_done, n + 1)
                else:
                    v.wait_ge(piece_used, N_PIECES)
                xh = xs[:, q // 2, HALF * (q % 2):HALF * (q % 2 + 1)]
                nc.vector.tensor_tensor(xh, bank[4 + q][:, :], xh, ALU.add).then_inc(x_ready, 1)
            for j in (0, 1):
                v.wait_ge(tp_done, 8 + j + 1)
                nc.vector.tensor_copy(xT[:, 2 * j:2 * j + 2, :],
                                      bank[j][:, :].rearrange("p (k t) -> p k t", k=2)).then_inc(tp_evac, 1)
            for b in range(TB):
                square_sum(1, b, 3 + b)
            v.wait_ge(gffn_loaded, 16)
            for b in range(TB):
                inverse(1, b)
                nc.vector.scalar_tensor_tensor(out=hs[:, b, :], in0=xs[:, b, :], scalar=rstd[:, b:b + 1],
                                               in1=gffn, op0=ALU.mult, op1=ALU.mult).then_inc(h_ready, 1)
            v.wait_ge(iota_ready, 1)
            v.wait_ge(router_done, 1)
            routed = [0]

            def link(ins):
                ins.then_inc(routing, 1)
                routed[0] += 1
                v.wait_ge(routing, routed[0])

            for b in range(TB):
                ins = nc.vector.scalar_tensor_tensor(out=lg[:, b, 0:NE], in0=bank[3][:, b * NE:(b + 1) * NE],
                                                     scalar=rstd[:, b:b + 1], in1=br, op0=ALU.mult, op1=ALU.add)
            link(ins)
            for b in range(TB):
                ins = nc.vector.max(top8[:, b, :], lg[:, b, 0:NE])
            link(ins)
            nc.vector.tensor_scalar(nlmax, top8[:, :, 0], -1.0, None, ALU.mult).then_inc(nlmax_ready, 1)
            link(nc.vector.tensor_copy(rep8[:, :, 0:TOPE], top8[:, :, 0:TOPE]))
            for b in range(TB):
                ins = nc.vector.match_replace(lgt[:, b, :], rep8[:, b, :], lg[:, b, :], TAKEN)
            link(ins)
            link(nc.vector.tensor_scalar(emask, lgt[:, :, 0:NE], (MASKED + TAKEN) / 2, None, ALU.is_lt))
            assert routed[0] == R_MASK
            v.wait_ge(eexp_ready, 2)
            link(nc.vector.tensor_tensor(eexp, eexp, emask, ALU.mult))
            link(nc.vector.tensor_reduce(lsum, eexp, X, ALU.add))
            link(nc.vector.reciprocal(linv, lsum))
            for b in range(TB):
                ins = nc.vector.tensor_scalar(comb[:, b, 0:NE], eexp[:, b, :], linv[:, b:b + 1], None, ALU.mult)
            link(ins)
            assert routed[0] == R_COMB
            v.wait_ge(rank_done, 1)
            link(nc.vector.scalar_tensor_tensor(out=posn[:, :, 0:NE],
                                                in0=bank[2][:, 0:2 * NE].rearrange("p (b e) -> p b e", b=2),
                                                scalar=1.0, in1=emask, op0=ALU.add, op1=ALU.mult))

            def make_picks(e):
                for b in range(TB):
                    for i in range(2):
                        ins = nc.vector.tensor_scalar(pick[:, b, i * SLOTS:(i + 1) * SLOTS], iota_r,
                                                      posn[:, b, bass.ds(e + i, 1)], None, ALU.is_equal)
                ins.then_inc(pick_ready, 1)

            def experts_round(r):
                if not isinstance(r, int):
                    v.wait_ge(scattered, r * (4 * PAIRS))
                    nc.vector.tensor_scalar(iota_r, iota_r, float(SLOTS), None, ALU.add).then_inc(iota_ready, 1)
                    v.wait_ge(iota_ready, r + 1)
                make_picks(0)
                if isinstance(r, int):
                    v.wait_ge(counts_done, 1)
                    link(nc.vector.tensor_reduce(cmax, bank[3][0:1, 0:NE], X, ALU.max))
                    assert routed[0] == R_COUNT
                    nc.vector.tensor_copy(count, cmax).then_inc(count_ready, 1)
                with v.Fori(0, NE // GROUP) as g:
                    for i in range(GROUP):
                        e = g * GROUP + i
                        u = r * NE + e
                        if i % 2 == 0:
                            v.wait_ge(gather_done, r * (2 * PAIRS + 2) + e + 2)
                            for b in range(TB):
                                for j in range(2):
                                    ins = nc.vector.tensor_scalar(gpick[:, b, j * SLOTS:(j + 1) * SLOTS], iota_r,
                                                                  posn[:, b, bass.ds(e + j, 1)],
                                                                  comb[:, b, bass.ds(e + j, 1)],
                                                                  ALU.is_equal, ALU.mult)
                            ins.then_inc(gpick_ready, 1)
                            make_picks(e + 2)
                        v.wait_ge(chunks_used, u * CHUNKS + KD)
                        nc.vector.tensor_scalar(gclip, GA[:, :], LIMIT, None, ALU.min).then_inc(gclip_ready, 1)
                        nc.vector.tensor_scalar(uclip, UA[:, :], LIMIT, -LIMIT, ALU.min, ALU.max).then_inc(uclip_ready, 1)
                        v.wait_ge(uclip_ready, u + 1)
                        nc.vector.scalar_tensor_tensor(out=uclip, in0=uclip, scalar=1.0, in1=gclip,
                                                       op0=ALU.add, op1=ALU.mult).then_inc(gu_ready, 1)
                        v.wait_ge(sig_ready, u + 1)
                        v.wait_ge(gu_ready, u + 1)
                        nc.vector.tensor_tensor(act, uclip, act, ALU.mult).then_inc(act_ready, 1)
                        make_sel(e + 1)
                        v.wait_ge(chunks_used, u * CHUNKS + CHUNKS)
                        own = slice((i % 2) * SLOTS, (i % 2 + 1) * SLOTS)
                        nc.vector.tensor_copy(ys[own, 1, :], YT[SLOTS:2 * SLOTS, :]).then_inc(y1_ready, 1)

            experts_round(0)
            v.wait_ge(count_ready, 1)
            most = v.value_load(count[0:1, 0:1], min_val=0, max_val=SEQ)
            with v.If(most > SLOTS):
                with v.Fori(1, ROUNDS) as r:
                    experts_round(r)
            v.wait_ge(gfin_loaded, 16)
            square_sum(2, 0, 2)
            inverse(2, 0)
            result(0, 0)
            square_sum(2, 1, 4)
            result(0, 1)
            inverse(2, 1)
            result(1, 0)
            result(1, 1)

        @block.tensor
        def _(pe):
            mm = nc.tensor.matmul

            def transposes(src, columns, ready):
                for c in columns:
                    for b in range(TB):
                        pe.wait_ge(*ready(b, c))
                        for j in (2 * c, 2 * c + 1):
                            for k in (2 * j, 2 * j + 1):
                                o = (k % 2) * SEQ + b * P
                                ins = nc.tensor.transpose(bank[j][:, o:o + P], src[:, b, k * P:(k + 1) * P], ident)
                            if b == TB - 1:
                                ins.then_inc(tp_done, 1)

            def tok(t, k, b):
                return t[:, k, b * P:(b + 1) * P]

            def three(o, ah, al, bh, bl, start, stop, first_in_bank=True):
                mm(o, ah, bh, start=start and first_in_bank, stop=False, skip_group_check=True)
                mm(o, ah, bl, start=False, stop=False, skip_group_check=True)
                return mm(o, al, bh, start=False, stop=stop, skip_group_check=True)

            def piece_idx(n):
                h, l = piece_cols(wh[:, n % LOOK, :], n), piece_cols(wl[:, n % LOOK, :], n)
                for i in range(2):
                    k = 2 * (n - P_IDX) + i
                    for blk, (bk, c0) in enumerate(((bank[4], 0), (bank[4], SEQ), (bank[5], 0))):
                        c = slice(blk * P, (blk + 1) * P)
                        ins = three(bk[:, c0:c0 + SEQ], h[:, i, c], l[:, i, c], hTh[:, k, :], hTl[:, k, :],
                                    k == 0, k == KD - 1, c0 == 0)
                ins.then_inc(piece_used, 1)

            def piece_group(n):
                g, kp = (n - P_Q) // 4, (n - P_Q) % 4
                h, l = piece_cols(wh[:, n % LOOK, :], n), piece_cols(wl[:, n % LOOK, :], n)
                if g >= 2 and kp == 0:
                    pe.wait_ge(half_evac, 2 * (g - 1))
                for i in range(2):
                    k = 2 * kp + i
                    st, sp_ = k == 0, k == KD - 1
                    if g < 2:
                        for blk in range(4):
                            c = slice(blk * P, (blk + 1) * P)
                            ins = three(bank[2 * (g % 2) + blk // 2][:, (blk % 2) * SEQ:(blk % 2 + 1) * SEQ],
                                        h[:, i, c], l[:, i, c], hTh[:, k, :], hTl[:, k, :], st, sp_, blk % 2 == 0)
                    else:
                        for b in range(TB):
                            ins = three(bank[2 * (g % 2) + b][:, :], tok(hTh, k, b), tok(hTl, k, b),
                                        h[:, i, :], l[:, i, :], st, sp_)
                ins.then_inc(piece_used, 1)

            def piece_product(n, n0, nk, ah, al, banks, done, order):
                k = n - n0
                h, l = wh[:, n % LOOK, :], wl[:, n % LOOK, :]
                for i, q in enumerate(order):
                    if n == P_BP:
                        pe.wait_ge(half_evac, 14 if q < 2 else 16)
                    if n == P_WO:
                        pe.wait_ge(gated, 4 + i + 1)
                    b, c = q // 2, slice((q % 2) * HALF, (q % 2 + 1) * HALF)
                    ins = three(banks[q][:, :], tok(ah, k, b), tok(al, k, b), h[:, c], l[:, c], k == 0, k == nk - 1)
                    if k == nk - 1 and i < 3:
                        ins.then_inc(done, 1)
                ins.then_inc(piece_used, 1)

            def attention_branch():
                for c in range(2):
                    for k in range(4):
                        n = P_BA + k
                        if c == 0:
                            pe.wait_ge(low_ready, n + 1)
                        h, l = wh[:, n % LOOK, c * HALF:(c + 1) * HALF], wl[:, n % LOOK, c * HALF:(c + 1) * HALF]
                        for b in range(TB):
                            ins = three(bank[4 + 2 * b + c][:, :], tok(atth, k, b), tok(attl, k, b), h, l, k == 0, k == 3)
                            if k == 3 and (b, c) != (1, 1):
                                ins.then_inc(branch_done, 1)
                        if c:
                            ins.then_inc(piece_used, 1)
                            if k == 2:
                                transposes(hs, (0,), lambda b, c: (merged, b + 1))

            def indexer_scores():
                pe.wait_ge(idx_ready, 4)
                for b in range(TB):
                    nc.tensor.transpose(bank[5][:, 3 * P + NIH * b:3 * P + NIH * (b + 1)], wiT[:, b * P:(b + 1) * P],
                                        ident[DI:DI + NIH, DI:DI + NIH])
                for b in range(TB):
                    for i in range(NIH):
                        r, c = DI * (i % 2), SEQ * (i // 2)
                        ins = mm(bank[4 + 2 * b + i % 2][:, c:c + P * (b + 1)], qiT[r:r + DI, i // 2, b * P:(b + 1) * P],
                                 kiT[r:r + DI, 0:P * (b + 1)], start=True, stop=True)
                    ins.then_inc(sc_done, 1)

            def pooling():
                pe.wait_ge(half_evac, 8)
                pe.wait_ge(band_loaded, 16)
                pe.wait_ge(relu_ready, 4)
                for g in range(4):
                    ug, bk, c = slice(g * P, (g + 1) * P), bank[4 + g // 2], (g % 2) * SEQ
                    mm(bk[:, c:c + P], uu[:, 0, ug], band[:, 3 * g, :], start=True, stop=True)
                    mm(bk[:, c + P:c + SEQ], uu[:, 0, ug], band[:, 3 * g + 1, :], start=True, stop=False)
                    ins = mm(bk[:, c + P:c + SEQ], uu[:, 1, ug], band[:, 3 * g + 2, :], start=False, stop=True)
                    if g % 2:
                        ins.then_inc(pool_done, 1)

            def mixing():
                pe.wait_ge(poolw_loaded, 32)
                for g in range(4):
                    pe.wait_ge(pool_evac, 1 + g // 2)
                    ins = mm(bank[4 + g // 2][:, (g % 2) * SEQ:(g % 2 + 1) * SEQ], poolw[:, g, :], pooledT[:, g, :],
                             start=True, stop=True)
                    if g % 2:
                        ins.then_inc(pool_done, 1)

            def logits(p):
                if p == 0:
                    pe.wait_ge(half_evac, 4)
                    pe.wait_ge(relu_ready, 4)
                else:
                    pe.wait_ge(logit_read, 2 * p)
                half = (slice(0, DH), slice(DH, 2 * DH))
                for i in range(2):
                    mm(bank[6 + i][:, 0:P], qT[half[i], p, 0:P], kT[half[i], p, 0:P], start=True, stop=True)
                for i in range(2):
                    mm(bank[6 + i][:, P:P + SEQ], qT[half[i], p, P:SEQ], kT[half[i], p, :], start=True, stop=True)\
                        .then_inc(logit_done, 1)

            def transpose_probs(h):
                pe.wait_ge(prob_ready, h + 1)
                if h == 0:
                    pe.wait_ge(mix_low, 4)
                else:
                    pe.wait_ge(pT_ready, h)
                for i in range(3):
                    ins = nc.tensor.transpose(bank[4][:, i * P:(i + 1) * P], prob[:, h % 2, i * P:(i + 1) * P], ident)
                ins.then_inc(pT_done, 1)

            def values(p):
                if p >= 1:
                    pe.wait_ge(att_low, p)
                for i in range(2):
                    pe.wait_ge(pT_ready, 2 * p + i + 1)
                    c = slice((2 * p + i) * DH, (2 * p + i + 1) * DH)
                    mm(bank[5][i * DH:(i + 1) * DH, 0:SEQ], vv[:, 0, c], pT[:, i, 0:SEQ], start=True, stop=False)
                for i in range(2):
                    c = slice((2 * p + i) * DH, (2 * p + i + 1) * DH)
                    mm(bank[5][i * DH:(i + 1) * DH, P:SEQ], vv[:, 1, c], pT[:, i, SEQ:SEQ + P], start=False, stop=True)\
                        .then_inc(pv_done, 1)

            pe.wait_ge(cst_loaded, 16)
            transposes(hs, (0, 1), lambda b, c: (h_ready, b + 1))
            for n in range(N_PIECES):
                if n == P_Q + 1:
                    indexer_scores()
                if n in (20, 24, 28, 32):
                    logits((n - 20) // 4)
                if n == P_BA:
                    pe.wait_ge(att_low, 4)
                    pe.wait_ge(logit_read, NH)
                    attention_branch()
                    continue
                if P_BA < n < P_WO:
                    continue
                if n == P_WO:
                    pe.wait_ge(tp_low, 6)
                if n == P_WO + 2:
                    transposes(hs, (1,), lambda b, c: (merged, 2 + b + 1))
                if n == P_WO + 4:
                    pe.wait_ge(tp_low, 8)
                pe.wait_ge(low_ready, n + 1)
                if n < P_Q:
                    pe.wait_ge(tp_low, n + 1)
                    piece_idx(n)
                elif n < P_BP:
                    piece_group(n)
                elif n < P_BA:
                    piece_product(n, P_BP, 4, mixh, mixl, bank[0:4], branch_done, range(4))
                else:
                    piece_product(n, P_WO, 8, hTh, hTl, bank[4:8], wo_done, ORDER)
                if n == 1:
                    pe.wait_ge(table_loaded, 32)
                    mm(bank[6][0:NH, 0:SEQ], table, hot, start=True, stop=True).then_inc(skew_done, 1)
                elif n == 21:
                    pooling()
                elif n == 23:
                    mixing()
                q, p = n % 4, n // 4
                if 24 <= n < 39:
                    if q in (0, 1):
                        transpose_probs(2 * (p - 6) + q)
                    elif q == 2:
                        values(p - 6)
            lo, hi = slice(0, SLOTS), slice(SLOTS, 2 * SLOTS)

            def bias1(bk, q0):
                for q, part in ((q0, lo), (q0 + 1, hi)):
                    rows = slice(q * NE, (q + 1) * NE)
                    mm(bk[part, :], sel[rows, :], b1s[rows, :], start=True, stop=False)

            def residual(q):
                mm(YSUM[q][:, :], ident, xs[:, q // 2, HALF * (q % 2):HALF * (q % 2 + 1)], start=True, stop=False,
                   skip_group_check=True)

            transposes(xs, (0, 1), lambda b, c: (x_ready, 2 * c + b + 1))
            residual(0)
            residual(2)
            pe.wait_ge(wr_ready, 1)
            for k in range(KD):
                if k % 4 == 0:
                    pe.wait_ge(tp_evac, 4)
                o = bank[2][(k % 4) * NE:(k % 4 + 1) * NE, 0:SEQ]
                ins = mm(o, wr[:, k, :], xT[:, k, :], start=k < 4, stop=k >= 4)
            ins.then_inc(parts_done, 1)
            pe.wait_ge(sel_ready, 1)
            pe.wait_ge(b1_loaded, 16)
            bias1(GA, 0)
            pe.wait_ge(parts_ready, 1)
            for b in range(TB):
                ins = mm(bank[3][:, b * NE:(b + 1) * NE], parts[:, b * P:(b + 1) * P], fold[:, 0:NE], start=True, stop=True)
            ins.then_inc(router_done, 1)
            bias1(UA, 2)
            residual(1)
            pe.wait_ge(routing, R_MASK)
            mm(bank[2][:, 0:NE], tri, emask[:, 0, :], start=True, stop=True)
            mm(bank[2][:, NE:2 * NE], ones, emask[:, 0, :], start=True, stop=False)
            mm(bank[2][:, NE:2 * NE], tri, emask[:, 1, :], start=False, stop=True).then_inc(rank_done, 1)
            for b in range(TB):
                ins = mm(bank[3][:, 0:NE], ones, emask[:, b, :], start=b == 0, stop=b == 1)
            ins.then_inc(counts_done, 1)
            residual(3)

            def gather(h):
                for k in range(4):
                    d = slice((4 * h + k) * P, (4 * h + k + 1) * P)
                    for b in range(TB):
                        ins = mm(GATHER[:, k * P:(k + 1) * P], hs[:, b, d], pick[:, b, :],
                                 start=b == 0, stop=b == TB - 1)
                ins.then_inc(gather_done, 1)

            def loaded_chunk(u4, c, written_out):
                i, loads, _ = plan[c] if written_out else slots[c % ERING]
                if written_out:
                    pe.wait_ge(chunk_loaded[i], 16 * loads)
                else:
                    pe.wait_ge(chunk_loaded[i], u4 * (16 * TURNS) + 16 * (loads + c // ERING + 1 - TURNS))
                return place[i]

            def expert(r, g, i):
                e = g * GROUP + i
                u, u4 = r * NE + e, r * (NE // GROUP) + g
                written_out = isinstance(g, int)
                pair = g * (GROUP // 2) + i // 2
                own = slice((i % 2) * SLOTS, (i % 2 + 1) * SLOTS)
                for k in range(KD):
                    if i % 2 == 0 and k % 4 == 0:
                        if written_out and i == 0 and k == 4:
                            gather(1)
                        pe.wait_ge(xgT_ready, r * (2 * PAIRS + 2) + 2 * pair + k // 4 + 1)
                    w = loaded_chunk(u4, i * CHUNKS + k, written_out)
                    for bk, c in ((GA, 0), (UA, F)):
                        for part, c1 in ((lo, c), (hi, c + HALF)):
                            ins = mm(bk[part, :], xgT[i // 2 % 2][:, k, own], w[:, c1:c1 + HALF],
                                     start=False, stop=k == KD - 1)
                    ins.then_inc(chunks_used, 1)
                if written_out:
                    if i == 0:
                        pe.wait_ge(combT_ready, 2)
                        pe.wait_ge(b2_loaded, 16)
                    rows = slice((i % 2) * NE, (i % 2 + 1) * NE)
                    mm(YSUM[i][:, :], combT[rows, (i // 2) * P:(i // 2 + 1) * P], b2s[rows, :],
                       start=False, stop=True, skip_group_check=True)
                if i % 2 == 0:
                    pe.wait_ge(gpick_ready, r * PAIRS + pair + 1)
                    for b in range(TB):
                        ins = nc.tensor.transpose(YT[:, b * P:(b + 1) * P], gpick[:, b, :], ident)
                    ins.then_inc(gT_done, 1)
                    pe.wait_ge(pick_ready, r * (PAIRS + 1) + pair + 2)
                else:
                    pe.wait_ge(xgT_ready, r * (2 * PAIRS + 2) + 2 * pair + 3)
                gather(i % 2)
                pe.wait_ge(act_ready, u + 1)
                for c in range(4):
                    ins = nc.tensor.transpose(GA[:, c * P:(c + 1) * P], act[:, c * P:(c + 1) * P], ident)
                ins.then_inc(actT_done, 1)
                pe.wait_ge(sel_ready, u + 2)
                bias1(UA, 2)
                if i % 2 == 0:
                    pe.wait_ge(gT_ready, r * PAIRS + pair + 1)
                else:
                    pe.wait_ge(y_ready, u)
                    pe.wait_ge(y1_ready, u)
                pe.wait_ge(actT_ready, u + 1)
                for j in range(KD, CHUNKS):
                    w = loaded_chunk(u4, i * CHUNKS + j, written_out).rearrange("p (k n) -> p k n", k=2)
                    for kk in range(2):
                        k = 2 * (j - KD) + kk
                        a_k = actT[:, (k % 4) * P + (k // 4) * SLOTS:(k % 4) * P + (k // 4 + 1) * SLOTS]
                        for part, c1 in ((lo, 0), (hi, HALF)):
                            ins = mm(YT[part, :], a_k, w[:, kk, c1:c1 + HALF], start=k == 0, stop=k == KD - 1)
                    ins.then_inc(chunks_used, 1)
                bias1(GA, 0)
                if i % 2:
                    pe.wait_ge(y_ready, u + 1)
                    pe.wait_ge(y1_ready, u + 1)
                    for b in range(TB):
                        for c in range(2):
                            mm(YSUM[2 * b + c][:, :], gT[:, b * P:(b + 1) * P], ys[:, c, :],
                               start=False, stop=True, skip_group_check=True).then_inc(scattered, 1)

            pe.wait_ge(pick_ready, 1)
            gather(0)
            pe.wait_ge(routing, R_COUNT)
            for b in range(TB):
                ins = nc.tensor.transpose(bank[3][0:NE, b * P:(b + 1) * P], comb[:, b, 0:NE], ident)
            ins.then_inc(combT_done, 1)
            for i in range(GROUP):
                expert(0, 0, i)
            with pe.Fori(1, NE // GROUP) as g:
                for i in range(GROUP):
                    expert(0, g, i)
            pe.wait_ge(count_ready, 1)
            most = pe.value_load(count[0:1, 0:1], min_val=0, max_val=SEQ)
            with pe.If(most > SLOTS):
                with pe.Fori(1, ROUNDS) as r:
                    pe.wait_ge(pick_ready, r * (PAIRS + 1) + 1)
                    for h in range(2):
                        pe.wait_ge(xgT_ready, r * (2 * PAIRS + 2) + h)
                        gather(h)
                    with pe.Fori(0, NE // GROUP) as g:
                        for i in range(GROUP):
                            expert(r, g, i)


def constants():
    s = np.arange(P)[:, None]
    t = np.arange(P)[None, :]
    c = np.zeros((P, N_CONST), np.float32)
    c[:, K_ID:K_ID + P] = s == t
    c[:, K_TRI:K_TRI + P] = s < t
    c[:, K_ONE:K_ONE + P] = 1.0
    c[:, K_IOTA:K_IOTA + SLOTS] = np.arange(1, SLOTS + 1)
    c[:, K_FOLD:K_FOLD + NE + 1] = s % NE == t[:, 0:NE + 1] % NE
    for g, w in enumerate(POOL_WINDOWS):
        near = (t - s >= 0) & (t - s < w)
        blocks = (near / np.minimum(t + 1, w) - (s == t),
                  (P + t - s < w) / w,
                  near / w - (s == t))
        for i, m in enumerate(blocks):
            at = K_BAND + (3 * g + i) * P
            c[:, at:at + P] = m
    return c


def bucket_rows():
    hot = np.zeros((BUCKETS, SEQ), np.float32)
    exact = BUCKETS // 2
    for c in range(SEQ):
        n = SEQ - 1 - c
        big = exact + int(np.float32(math.log(max(n, 1) / exact) / math.log(MAX_DIST / exact) * (BUCKETS - exact)))
        hot[n if n < exact else min(big, BUCKETS - 1), c] = 1.0
    return hot


def kernel(x, mix_norm, w_in, pool_w, pool_scale, w_branch_pool, w_branch_attn, rel_bias, w_out, ffn_norm,
           w_router, b_router, w1, b1, w2, b2, final_norm):
    import concourse.bacc as bacc
    from concourse.bass_utils import run_bass_kernel_spmd

    arrays = {
        "x": x[0], "mix_cols": mix_norm[0].reshape(KD, P).T, "w_in": w_in[0], "pool_w": pool_w[0],
        "pool_scale": pool_scale[0].reshape(4, P).T, "w_branch_pool": w_branch_pool[0],
        "w_branch_attn": w_branch_attn[0], "rel_bias": rel_bias, "w_out": w_out[0],
        "ffn_norm": ffn_norm[0], "ffn_cols": ffn_norm[0].reshape(KD, P).T,
        "w_router": w_router[0], "b_router": b_router[0],
        "w1": w1[0], "b1": b1[0].reshape(NE, 4, HALF).transpose(1, 0, 2).reshape(4 * NE, HALF), "w2": w2[0],
        "b2": b2[0].reshape(NE, 2, HALF).transpose(1, 0, 2).reshape(2 * NE, HALF), "final_norm": final_norm,
        "consts": constants(), "bucket_hot": bucket_rows(),
    }
    arrays = {f"in_{n}": np.ascontiguousarray(a) for n, a in arrays.items()}
    nc = bacc.Bacc("TRN2", target_bir_lowering=False, num_devices=1)
    args = [nc.dram_tensor(n, a.shape, mybir.dt.from_np(a.dtype), kind="ExternalInput").ap() for n, a in arrays.items()]
    out = nc.dram_tensor("out", (SEQ, D), mybir.dt.float32, kind="ExternalOutput").ap()
    hybrid_block(nc, *args, out)
    r = run_bass_kernel_spmd(nc, [arrays], core_ids=[0])
    return r.results[0]["out"].reshape(1, SEQ, D)
```
